# Optimizing a Trainium2 kernel written in Bass

```python
import math
import jax
import jax.numpy as jnp
from jax import lax
import numpy as np

D_MODEL = 1024
BATCH = 1
SEQ = 1024
DEPTH = 1

GRID_W = 64
CTX_LEN = 256
N_MOD = 6
EPS = 1e-6

A_HEADS = 4
A_HEAD_DIM = 64
A_V_DIM = 2 * A_HEAD_DIM
A_WIDTH = A_HEADS * A_V_DIM
Q_BLOCK = 128
ROPE_THETA = 10000.0
SUBLN_EPS = 1e-5

CONV_CH = 512
CONV_K = 31

C_HEADS = 4
C_HEAD_DIM = 128
C_WIDTH = C_HEADS * C_HEAD_DIM
SHORT_K = 5
CHUNK = 64

N_BRANCH = 3
BRANCH_W = 512

A_COLS = 3 * A_WIDTH
C_COLS = 4 * C_WIDTH + 4 * C_HEADS
B_COLS = 2 * CONV_CH
GATE_COLS = N_BRANCH * D_MODEL
CTX_COLS = A_COLS + C_COLS
IN_COLS = A_COLS + C_COLS + B_COLS + GATE_COLS

N_EXPERTS = 16
N_GROUPS = 4
EXPERTS_PER_GROUP = N_EXPERTS // N_GROUPS
TOP_K = 2
D_EXPERT = 1024
MOE_BLOCK = 128

kernel_name = "hybrid_diffusion_prefix_trunk"

def rms_norm(x, w, eps=EPS):
    xf = x.astype(jnp.float32)
    y = xf * lax.rsqrt(jnp.mean(xf * xf, axis=-1, keepdims=True) + eps)
    return (y * w.astype(jnp.float32)).astype(x.dtype)

def layer_norm(x, w, b, eps=1e-5):
    xf = x.astype(jnp.float32)
    mu = jnp.mean(xf, axis=-1, keepdims=True)
    var = jnp.mean(jnp.square(xf - mu), axis=-1, keepdims=True)
    y = (xf - mu) * lax.rsqrt(var + eps)
    return (y * w.astype(jnp.float32) + b.astype(jnp.float32)).astype(x.dtype)

def l2_normalize(x, eps=1e-6):
    xf = x.astype(jnp.float32)
    return xf * lax.rsqrt(jnp.sum(xf * xf, axis=-1, keepdims=True) + eps)

def modulate(x, w, shift, scale):
    return rms_norm(x, w) * (1 + scale) + shift

def depthwise_conv(x, w):
    k = w.shape[0]
    return lax.conv_general_dilated(
        x, w[:, None, :].astype(x.dtype), window_strides=(1,), padding=[(k // 2, k // 2)],
        dimension_numbers=("NWC", "WIO", "NWC"), feature_group_count=x.shape[-1])

def axial_rope_tables(n_tokens):
    rows = n_tokens // GRID_W
    r, col = jnp.meshgrid(jnp.arange(rows, dtype=jnp.float32), jnp.arange(GRID_W, dtype=jnp.float32), indexing="ij")
    axis_dim = A_HEAD_DIM // 2
    inv_freq = ROPE_THETA ** (-jnp.arange(0, axis_dim, 2, dtype=jnp.float32) / axis_dim)
    ang_r = r.reshape(-1, 1) * inv_freq
    ang_c = col.reshape(-1, 1) * inv_freq
    shape = (n_tokens, 1, 1, axis_dim // 2)
    return (jnp.cos(ang_r).reshape(shape), jnp.sin(ang_r).reshape(shape),
            jnp.cos(ang_c).reshape(shape), jnp.sin(ang_c).reshape(shape))

def rope_rotate(x, cos, sin):
    x1, x2 = jnp.split(x, 2, axis=-1)
    cos = cos.astype(x.dtype)
    sin = sin.astype(x.dtype)
    return jnp.concatenate([x1 * cos - x2 * sin, x2 * cos + x1 * sin], axis=-1)

def apply_axial_rope(x, tabs):
    cos_r, sin_r, cos_c, sin_c = tabs
    x_row, x_col = jnp.split(x, 2, axis=-1)
    return jnp.concatenate([rope_rotate(x_row, cos_r, sin_r), rope_rotate(x_col, cos_c, sin_c)], axis=-1)

def diff_softmax_attend(q, k, v, lam):
    s = jnp.einsum("bhmqd,bhmkd->bhmqk", q, k, preferred_element_type=jnp.float32) * (A_HEAD_DIM ** -0.5)
    p = jax.nn.softmax(s, axis=-1)
    a = p[:, :, 0] - lam * p[:, :, 1]
    return jnp.einsum("bhqk,bhkd->bhqd", a.astype(v.dtype), v)

def diff_attn_branch(a_lat, a_ctx, rope, lambda_init, need_ctx, qn_w, kn_w, lam_p, subln_w):
    def heads(p):
        b, t, _ = p.shape
        q, k, v = jnp.split(p, 3, axis=-1)
        q = rms_norm(q.reshape(b, t, A_HEADS, 2, A_HEAD_DIM), qn_w)
        k = rms_norm(k.reshape(b, t, A_HEADS, 2, A_HEAD_DIM), kn_w)
        return q, k, v.reshape(b, t, A_HEADS, A_V_DIM)

    def to_bhm(t):
        return t.transpose(0, 2, 3, 1, 4)

    def finish(o):
        return (rms_norm(o, subln_w, SUBLN_EPS) * (1.0 - lambda_init)).reshape(o.shape[0], o.shape[1], A_WIDTH)

    lq, lk, lv = heads(a_lat)
    cq, ck, cv = heads(a_ctx)
    lq = apply_axial_rope(lq, rope)
    lk = apply_axial_rope(lk, rope)
    lp = lam_p.astype(jnp.float32)
    lam = jnp.exp(jnp.sum(lp[0] * lp[1])) - jnp.exp(jnp.sum(lp[2] * lp[3])) + lambda_init

    b, s = a_lat.shape[:2]
    nb = s // Q_BLOCK
    k_all = jnp.concatenate([to_bhm(ck), to_bhm(lk)], axis=3)
    v_all = jnp.concatenate([cv, lv], axis=1).transpose(0, 2, 1, 3)
    q_blocks = to_bhm(lq).reshape(b, A_HEADS, 2, nb, Q_BLOCK, A_HEAD_DIM).transpose(3, 0, 1, 2, 4, 5)
    o = lax.map(lambda qb: diff_softmax_attend(qb, k_all, v_all, lam), q_blocks)
    y_lat = finish(o.transpose(1, 0, 3, 2, 4).reshape(b, s, A_HEADS, A_V_DIM))
    if not need_ctx:
        return y_lat, None
    oc = diff_softmax_attend(to_bhm(cq), to_bhm(ck), cv.transpose(0, 2, 1, 3), lam)
    return y_lat, finish(oc.transpose(0, 2, 1, 3))

def conformer_conv(u, dw_w, dw_b, ln_w, ln_b):
    a, g = jnp.split(u, 2, axis=-1)
    y = a * jax.nn.sigmoid(g)
    y = depthwise_conv(y, dw_w) + dw_b.astype(y.dtype)
    return jax.nn.silu(layer_norm(y, ln_w, ln_b))

def gated_delta_chunked(q, k, v, g, beta, state, with_output):
    f32 = jnp.float32
    b, t, h, _ = q.shape
    n = t // CHUNK

    def chunks(x):
        return x.astype(f32).reshape(b, n, CHUNK, h, -1).transpose(1, 0, 3, 2, 4)

    q, k, v = chunks(q), chunks(k), chunks(v)
    g = jnp.cumsum(chunks(g[..., None])[..., 0], axis=-1)
    beta = chunks(beta[..., None])[..., 0]
    idx = jnp.arange(CHUNK)
    incl = idx[:, None] >= idx[None, :]
    strict = idx[:, None] > idx[None, :]
    diff = g[..., :, None] - g[..., None, :]
    decay = jnp.where(incl, jnp.exp(jnp.where(incl, diff, 0.0)), 0.0)
    kb = k * beta[..., None]
    lower = jnp.where(strict, jnp.einsum("nbhid,nbhjd->nbhij", kb, k) * decay, 0.0)
    eye = jnp.eye(CHUNK, dtype=f32)
    t_inv = lax.linalg.triangular_solve(lower + eye, jnp.broadcast_to(eye, lower.shape),
                                        left_side=True, lower=True, unit_diagonal=True)
    u = t_inv @ (v * beta[..., None])
    w = t_inv @ (kb * jnp.exp(g)[..., None])
    g_last = g[..., -1]
    k_dec = k * jnp.exp(g_last[..., None] - g)[..., None]

    def advance(s, u_i, w_i, kd_i, gl_i):
        v_new = u_i - w_i @ s
        s_next = s * jnp.exp(gl_i)[..., None, None] + jnp.swapaxes(kd_i, -1, -2) @ v_new
        return s_next, v_new

    if not with_output:
        def step_state(s, xs):
            return advance(s, *xs)[0], None
        state, _ = lax.scan(step_state, state, (u, w, k_dec, g_last))
        return None, state

    q_dec = q * jnp.exp(g)[..., None]
    intra = jnp.where(incl, jnp.einsum("nbhid,nbhjd->nbhij", q, k) * decay, 0.0)

    def step(s, xs):
        u_i, w_i, kd_i, gl_i, qd_i, a_i = xs
        s_next, v_new = advance(s, u_i, w_i, kd_i, gl_i)
        return s_next, qd_i @ s + a_i @ v_new

    state, o = lax.scan(step, state, (u, w, k_dec, g_last, q_dec, intra))
    return o.transpose(1, 0, 3, 2, 4).reshape(b, t, h, v.shape[-1]), state

def gdn_prepare(cols, conv_w, a_log, dt_bias):
    f32 = jnp.float32
    b, t, _ = cols.shape
    qkv = jax.nn.silu(depthwise_conv(cols[..., :3 * C_WIDTH], conv_w))
    q, k, v = jnp.split(qkv, 3, axis=-1)
    q = l2_normalize(q.reshape(b, t, C_HEADS, C_HEAD_DIM)) * (C_HEAD_DIM ** -0.5)
    k = l2_normalize(k.reshape(b, t, C_HEADS, C_HEAD_DIM))
    v = v.reshape(b, t, C_HEADS, C_HEAD_DIM).astype(f32)
    o = 4 * C_WIDTH
    beta = jax.nn.sigmoid(cols[..., o:o + 2 * C_HEADS].astype(f32)).reshape(b, t, 2, C_HEADS)
    a = cols[..., o + 2 * C_HEADS:].astype(f32).reshape(b, t, 2, C_HEADS)
    g = -jnp.exp(a_log.astype(f32)) * jax.nn.softplus(a + dt_bias.astype(f32))
    return q, k, v, g, beta

def gdn_gated_out(o, z, norm_w):
    b, t = z.shape[:2]
    y = rms_norm(o, norm_w) * jax.nn.silu(z.reshape(b, t, C_HEADS, C_HEAD_DIM).astype(jnp.float32))
    return y.reshape(b, t, C_WIDTH).astype(z.dtype)

def orient(x, direction):
    return jnp.flip(x, axis=1) if direction == 1 else x

def gdn_branch(c_lat, c_ctx, need_ctx, conv_w, a_log, dt_bias, norm_w):
    lat = gdn_prepare(c_lat, conv_w, a_log, dt_bias)
    ctx = gdn_prepare(c_ctx, conv_w, a_log, dt_bias)
    s0 = jnp.zeros((c_lat.shape[0], C_HEADS, C_HEAD_DIM, C_HEAD_DIM), jnp.float32)
    o_lat, o_ctx = 0.0, 0.0
    for d in range(2):
        def seqs(pack):
            q, k, v, g, beta = pack
            return [orient(x, d) for x in (q, k, v, g[:, :, d], beta[:, :, d])]
        oc, s_ctx = gated_delta_chunked(*seqs(ctx), s0, need_ctx)
        ol, _ = gated_delta_chunked(*seqs(lat), s_ctx, True)
        o_lat = o_lat + orient(ol, d)
        if need_ctx:
            o_ctx = o_ctx + orient(oc, d)
    y_lat = gdn_gated_out(o_lat, c_lat[..., 3 * C_WIDTH:4 * C_WIDTH], norm_w)
    if not need_ctx:
        return y_lat, None
    return y_lat, gdn_gated_out(o_ctx, c_ctx[..., 3 * C_WIDTH:4 * C_WIDTH], norm_w)

def merge_branches(ys, gate_logits, w_branch, w_out):
    d = w_out.shape[0]
    gates = jax.nn.sigmoid(gate_logits)
    m = 0.0
    for i, y in enumerate(ys):
        m = m + gates[..., i * d:(i + 1) * d] * (y.astype(w_branch.dtype) @ w_branch[i])
    return m @ w_out

def route(h, router_w, router_bias):
    scores = jax.nn.sigmoid((h @ router_w).astype(jnp.float32))
    grp = (scores + router_bias.astype(jnp.float32)).reshape(-1, N_GROUPS, EXPERTS_PER_GROUP)
    best = jnp.argmax(lax.top_k(grp, TOP_K)[0].sum(-1), axis=-1)
    in_grp = jnp.take_along_axis(grp, best[:, None, None], axis=1)[:, 0]
    _, local = lax.top_k(in_grp, TOP_K)
    expert = best[:, None] * EXPERTS_PER_GROUP + local
    w = jnp.take_along_axis(scores, expert, axis=-1)
    return expert, w / jnp.sum(w, axis=-1, keepdims=True)

def moe_ffn(h, router_w, router_bias, w_gate, w_up, w_down):
    n, d = h.shape
    expert, gate = route(h, router_w, router_bias)
    n_assign = n * TOP_K
    flat_e = expert.reshape(-1)
    order = jnp.argsort(flat_e)
    sorted_e = flat_e[order]
    tok = order // TOP_K
    counts = jnp.zeros((N_EXPERTS,), jnp.int32).at[flat_e].add(1)
    padded = (counts + MOE_BLOCK - 1) // MOE_BLOCK * MOE_BLOCK
    pad_end = jnp.cumsum(padded)
    seg_start = jnp.cumsum(counts) - counts
    dest = (pad_end - padded)[sorted_e] + jnp.arange(n_assign) - seg_start[sorted_e]
    n_blocks = -(-n_assign // MOE_BLOCK) + N_EXPERTS
    rows = jnp.zeros((n_blocks * MOE_BLOCK, d), h.dtype).at[dest].set(h[tok])
    blk_expert = jnp.minimum(jnp.searchsorted(pad_end, jnp.arange(n_blocks) * MOE_BLOCK, side="right"), N_EXPERTS - 1)

    def expert_block(args):
        xb, e = args
        return (jax.nn.silu(xb @ w_gate[e]) * (xb @ w_up[e])) @ w_down[e]

    y = lax.map(expert_block, (rows.reshape(n_blocks, MOE_BLOCK, d), blk_expert)).reshape(-1, d)
    contrib = y[dest] * gate.reshape(-1)[order][:, None].astype(y.dtype)
    return jnp.zeros_like(h).at[tok].add(contrib)

def setup_inputs(seed: int = 0) -> dict:
    key = jax.random.key(seed)
    ks = jax.random.split(key, 32)
    f32 = jnp.float32
    D = D_MODEL

    def nrm(k, shape, scale):
        return jax.random.normal(k, shape, f32) * scale

    dt = jnp.exp(jax.random.uniform(ks[19], (DEPTH, 2, C_HEADS), f32, math.log(1e-3), math.log(1e-1)))
    return {
        "x": nrm(ks[0], (BATCH, SEQ, D), 1.0),
        "c": nrm(ks[1], (BATCH, D), 1.0),
        "ctx": nrm(ks[2], (BATCH, CTX_LEN, D), 1.0),
        "c_ctx": nrm(ks[3], (D,), 1.0),
        "w_mod": nrm(ks[4], (DEPTH, D, N_MOD * D), 0.5 * D ** -0.5),
        "b_mod": nrm(ks[5], (DEPTH, N_MOD * D), 0.02),
        "norm1_w": 1.0 + nrm(ks[6], (DEPTH, D), 0.05),
        "norm2_w": 1.0 + nrm(ks[7], (DEPTH, D), 0.05),
        "w_in": nrm(ks[8], (DEPTH, D, IN_COLS), D ** -0.5),
        "qn_w": 1.0 + nrm(ks[9], (DEPTH, A_HEAD_DIM), 0.05),
        "kn_w": 1.0 + nrm(ks[10], (DEPTH, A_HEAD_DIM), 0.05),
        "lam_p": nrm(ks[11], (DEPTH, 4, A_HEAD_DIM), 0.1),
        "subln_w": 1.0 + nrm(ks[12], (DEPTH, A_V_DIM), 0.05),
        "conv_dw_w": nrm(ks[13], (DEPTH, CONV_K, CONV_CH), CONV_K ** -0.5),
        "conv_dw_b": nrm(ks[14], (DEPTH, CONV_CH), 0.02),
        "conv_ln_w": 1.0 + nrm(ks[15], (DEPTH, CONV_CH), 0.05),
        "conv_ln_b": nrm(ks[16], (DEPTH, CONV_CH), 0.02),
        "gdn_conv_w": nrm(ks[17], (DEPTH, SHORT_K, 3 * C_WIDTH), SHORT_K ** -0.5),
        "gdn_a_log": jnp.log(jax.random.uniform(ks[18], (DEPTH, 2, C_HEADS), f32, 1.0, 16.0)),
        "gdn_dt_bias": jnp.log(jnp.expm1(dt)),
        "gdn_norm_w": 1.0 + nrm(ks[20], (DEPTH, C_HEAD_DIM), 0.05),
        "w_branch": nrm(ks[21], (DEPTH, N_BRANCH, BRANCH_W, D), BRANCH_W ** -0.5),
        "w_out": nrm(ks[22], (DEPTH, D, D), D ** -0.5),
        "router_w": nrm(ks[23], (D, N_EXPERTS), D ** -0.5),
        "router_bias": nrm(ks[24], (N_EXPERTS,), 0.01),
        "w_gate": nrm(ks[25], (DEPTH, N_EXPERTS, D, D_EXPERT), D ** -0.5),
        "w_up": nrm(ks[26], (DEPTH, N_EXPERTS, D, D_EXPERT), D ** -0.5),
        "w_down": nrm(ks[27], (DEPTH, N_EXPERTS, D_EXPERT, D), D_EXPERT ** -0.5),
    }

def reference(x, c, ctx, c_ctx, w_mod, b_mod, norm1_w, norm2_w, w_in, qn_w, kn_w, lam_p, subln_w,
              conv_dw_w, conv_dw_b, conv_ln_w, conv_ln_b, gdn_conv_w, gdn_a_log, gdn_dt_bias, gdn_norm_w,
              w_branch, w_out, router_w, router_bias, w_gate, w_up, w_down):
    b, s, d = x.shape
    rope = axial_rope_tables(s)
    silu_c = jax.nn.silu(c)
    silu_cc = jax.nn.silu(c_ctx)
    h_ctx = ctx
    for l in range(DEPTH):
        need_ctx = l < DEPTH - 1
        lambda_init = 0.8 - 0.6 * math.exp(-0.3 * l)
        sh1, sc1, g1, sh2, sc2, g2 = [m[:, None, :] for m in jnp.split(silu_c @ w_mod[l] + b_mod[l], N_MOD, axis=-1)]
        csh1, csc1, cg1, csh2, csc2, cg2 = jnp.split(silu_cc @ w_mod[l] + b_mod[l], N_MOD, axis=-1)

        p_lat = modulate(x, norm1_w[l], sh1, sc1) @ w_in[l]
        w_in_ctx = w_in[l] if need_ctx else w_in[l][:, :CTX_COLS]
        p_ctx = modulate(h_ctx, norm1_w[l], csh1, csc1) @ w_in_ctx
        o_a, o_c, o_b = A_COLS, A_COLS + C_COLS, A_COLS + C_COLS + B_COLS
        ya_l, ya_c = diff_attn_branch(p_lat[..., :o_a], p_ctx[..., :o_a], rope, lambda_init, need_ctx,
                                      qn_w[l], kn_w[l], lam_p[l], subln_w[l])
        yc_l, yc_c = gdn_branch(p_lat[..., o_a:o_c], p_ctx[..., o_a:o_c], need_ctx,
                                gdn_conv_w[l], gdn_a_log[l], gdn_dt_bias[l], gdn_norm_w[l])
        yb_l = conformer_conv(p_lat[..., o_c:o_b], conv_dw_w[l], conv_dw_b[l], conv_ln_w[l], conv_ln_b[l])
        x = x + g1 * merge_branches((ya_l, yb_l, yc_l), p_lat[..., o_b:], w_branch[l], w_out[l])
        if need_ctx:
            yb_c = conformer_conv(p_ctx[..., o_c:o_b], conv_dw_w[l], conv_dw_b[l], conv_ln_w[l], conv_ln_b[l])
            h_ctx = h_ctx + cg1 * merge_branches((ya_c, yb_c, yc_c), p_ctx[..., o_b:], w_branch[l], w_out[l])

        h2 = modulate(x, norm2_w[l], sh2, sc2).reshape(-1, d)
        if need_ctx:
            h2c = modulate(h_ctx, norm2_w[l], csh2, csc2).reshape(-1, d)
            f = moe_ffn(jnp.concatenate([h2, h2c], axis=0), router_w, router_bias, w_gate[l], w_up[l], w_down[l])
            x = x + g2 * f[:b * s].reshape(b, s, d)
            h_ctx = h_ctx + cg2 * f[b * s:].reshape(b, -1, d)
        else:
            x = x + g2 * moe_ffn(h2, router_w, router_bias, w_gate[l], w_up[l], w_down[l]).reshape(b, s, d)
    return x


_drawn_inputs = setup_inputs


def setup_inputs(seed=0):
    import zlib

    import numpy as np

    out = dict(_drawn_inputs(seed))
    spreads = {}
    factors = {'norm1_w': 3.31,
     'qn_w': 6.477,
     'kn_w': 8.0,
     'lam_p': 3.974,
     'subln_w': 17.992,
     'conv_dw_b': 29.195,
     'conv_ln_w': 17.273,
     'conv_ln_b': 42.288,
     'gdn_norm_w': 4.936,
     'norm2_w': 3.508,
     'router_bias': 2.969}
    for name, (base, spread) in spreads.items():
        noise = np.random.default_rng([zlib.crc32(name.encode()), seed]).standard_normal(out[name].shape)
        drawn = base * np.exp(spread * noise) if base else spread * noise
        out[name] = jnp.asarray(drawn.astype(out[name].dtype))
    for name, factor in factors.items():
        out[name] = (out[name] * factor).astype(out[name].dtype)
    return out
```

```python
import math
from contextlib import ExitStack

import numpy as np
import concourse.bass as bass
from concourse import mybir

F32 = mybir.dt.float32
I32 = mybir.dt.int32
ALU = mybir.AluOpType
ACT = mybir.ActivationFunctionType
AX = mybir.AxisListType
ds = bass.ds

P = 128
D = 1024
KD = D // P
SEQ = 1024
CTX = 256
TOK = CTX + SEQ
HEADS = 4
BW = 512
KB = BW // P
EPS = 1e-6
LAMBDA_INIT = 0.8 - 0.6 * math.exp(-0.3 * 0)
GRID_W = 64
A_Q, A_K, A_V = 0, 512, 1024
C_Q, C_Z, C_BETA = 1536, 1536 + 1536, 1536 + 2048
B_A = C_BETA + 16
GATES = B_A + 1024
N_EXP = 16
N_BLK = 32
ROWS = N_BLK * P
CW = CTX + 4 + SEQ
LAT = CTX + 4
RAW = CW + 4

_names = ["ident", "rot", "blk", "ones", "tri", "cum0", "cum1", "neg0", "neg1"]
LEVELS = [1, 2, 4, 8, 16, 32, 64]
CONST = {n: i * P for i, n in enumerate(_names)}
CONST["lev0"] = len(_names) * P
CONST["lev1"] = CONST["lev0"] + len(LEVELS) * P
CONST_W = CONST["lev1"] + len(LEVELS) * P


def constant_table():
    i = np.arange(P)
    t = np.zeros((P, CONST_W), np.float32)

    def put(name, m, at=0):
        t[:, CONST[name] + at:CONST[name] + at + P] = m

    put("ident", np.eye(P))
    r = np.zeros((P, P))
    for m in range(P):
        if m % 32 < 16:
            r[m + 16, m] = -1.0
        else:
            r[m - 16, m] = 1.0
    put("rot", r)
    put("blk", (i[:, None] // 64 == i[None, :] // 64))
    put("ones", np.ones((P, P)))
    put("tri", i[:, None] < i[None, :])
    put("cum0", i[:, None] <= i[None, :])
    put("cum1", i[:, None] >= i[None, :])
    put("neg0", np.where(i[None, :] >= i[:, None], 0.0, -1e30))
    put("neg1", np.where(i[None, :] <= i[:, None], 0.0, -1e30))
    for n, s in enumerate(LEVELS):
        m = (i[None, :] // (2 * s) == i[:, None] // (2 * s)) & (i[None, :] // s % 2 == 1) & (i[:, None] // s % 2 == 0)
        put("lev0", m, n * P)
        put("lev1", m.T, n * P)
    return t


def rope_table():
    inv = np.float32(10000.0) ** (-np.arange(0, 32, 2, dtype=np.float32) / np.float32(32))
    tok = np.arange(SEQ)
    row, col = (tok // GRID_W).astype(np.float32), (tok % GRID_W).astype(np.float32)
    out = np.zeros((P, 2, SEQ), np.float32)
    for p in range(P):
        ang = (row if p % 64 < 32 else col) * inv[p % 16]
        out[p, 0], out[p, 1] = np.cos(ang), np.sin(ang)
    return out


class Core:

    def __init__(self, nc, dram):
        self.nc, self.dram, self.n = nc, dram, 0

    def sb(self, st, name, shape, dt=F32):
        self.n += 1
        return st.enter_context(self.nc.sbuf_tensor(f"{name}_{self.n}", shape, dt))

    def ps(self, st, name, shape, dt=F32):
        self.n += 1
        return st.enter_context(self.nc.psum_tensor(f"{name}_{self.n}", shape, dt))

    def col(self, name, c=0):
        at = VEC[name][0] + c
        return self.vec[:, at:at + 1]

    def c(self, name, at=0, n=P):
        return self.const[:, CONST[name] + at * P:CONST[name] + at * P + n]


class Signals:

    def __init__(self, nc, st, stage):
        self.nc, self.stage, self.by_name = nc, stage, {}
        st.callback(self.clear)

    def __call__(self, name, n=None):
        key = f"{self.stage}_{name}" + ("" if n is None else str(n))
        if key not in self.by_name:
            self.by_name[key] = self.nc.alloc_semaphore(key)
        return self.by_name[key]

    def clear(self):
        self.nc.clear_and_free_semaphores(list(self.by_name.values()))
        self.nc.all_engine_barrier()


class Chain:

    def __init__(self, eng, sem):
        self.eng, self.s, self.base, self.n, self.it, self.per = eng, sem, 0, 0, None, 0

    def enter(self, it, per):
        self.base, self.n, self.it, self.per = self.base + self.n, 0, it, per

    def leave(self, trips):
        assert self.n == self.per, f"steps in the loop: {self.n}, said {self.per}"
        self.base, self.n, self.it = self.base + self.per * trips, 0, None

    def then(self, ins):
        self.n += 1
        ins.then_inc(self.s, 1)

    def wait(self):
        if self.it is not None:
            self.eng.wait_ge(self.s, self.it * self.per + (self.base + self.n))
        elif self.base + self.n:
            self.eng.wait_ge(self.s, self.base + self.n)

    def run(self, ins):
        self.then(ins)
        self.wait()


class Pass:

    def __init__(self, s, eng, it, per):
        self.s, self.eng, self.it, self.per = s, eng, it, per

    def step(self, later):
        return Pass(self.s, self.eng, self.it + -later if later < 0 else self.it - later, self.per)

    def after(self, name, j=None):
        n = self.per[name]
        u = 16 if name.startswith("load") else 1
        self.eng.wait_ge(self.s(name), self.it * (n * u) + (n + (n if j is None else j + 1)) * u)

    def after_last(self, name, j=None):
        n = self.per[name]
        u = 16 if name.startswith("load") else 1
        self.eng.wait_ge(self.s(name), self.it * (n * u) + (n if j is None else j + 1) * u)


def credit(s, eng, per, *names):
    for name in names:
        eng.sem_inc(s(name), per[name] * (16 if name.startswith("load") else 1))


VEC = {}
_at = 0
for _n, _w in [("c", 8), ("c_ctx", 8), ("norm1_w", 8), ("norm2_w", 8), ("b_mod", 48), ("conv_dw_b", 4),
               ("conv_ln_w", 4), ("conv_ln_b", 4), ("subln_w", 1), ("gdn_norm_w", 1), ("qn_w", 1), ("kn_w", 1)]:
    VEC[_n] = (_at, _w)
    _at += _w
VEC_N = _at
PREP_SMALL = 16 * (len(VEC) + 2 + 6)


def prepare(k):
    nc, dr = k.nc, k.dram
    BY_ACT = 4
    with ExitStack() as st:
        s = Signals(nc, st, "prep")
        rows = k.sb(st, "vec_rows", [VEC_N, P])
        rows31 = k.sb(st, "conv_rows", [124, P])
        rows5 = k.sb(st, "gdn_rows", [60, P])
        small = k.sb(st, "small_rows", [1, 32 + 256])
        sig_c = k.sb(st, "sigmoid_c", [P, 16])
        silu_c = k.sb(st, "silu_c", [P, 16])
        wm = k.w_mod
        xt = [k.sb(st, f"x_tile{i}", [P, D]) for i in range(2)]
        sq = k.sb(st, "squares", [P, D])
        ssum = k.sb(st, "square_sum", [P, 10])
        root = k.sb(st, "root", [P, 10])
        rstd = k.sb(st, "rstd", [P, 10])
        xn = [k.sb(st, f"x_normed{i}", [P, D]) for i in range(2)]
        lamp = k.sb(st, "lam_products", [1, 128])
        lams = k.sb(st, "lam_sums", [1, 4])
        spread = k.sb(st, "rows_to_spread", [1, 33])
        p_vec = k.ps(st, "p_vec", [P, 512])
        p_mod = k.ps(st, "p_mod", [P, 512])
        p_x = [k.ps(st, f"p_x{i}", [P, D]) for i in range(2)]
        mod_row = k.sb(st, "mod_row", [2, 6 * D])
        p_row = [p_vec, p_mod]
        p_mod = p_x[0]
        p_g = k.ps(st, "p_g", [P, D])

        with nc.Block() as block:
            @block.sync
            def _(sp):
                sp.dma_start(k.const[:], dr["consts"]).then_inc(s("consts_loaded"), 16)
                n_small = 0
                for n, (at, w) in VEC.items():
                    for half in range(2 if n in ("qn_w", "kn_w") else 1):
                        dst = rows[at:at + 1, half * 64:half * 64 + 64] if n in ("qn_w", "kn_w") else rows[at:at + w, :]
                        src = dr[n] if len(dr[n].shape) == 2 else dr[n].rearrange("(a n) -> a n", a=1)
                        if n not in ("qn_w", "kn_w"):
                            src = src.rearrange("a (c p) -> (a c) p", p=P)
                        sp.dma_start(dst, src).then_inc(s("small_loaded"), 16)
                        n_small += 16
                for dst, src in ((rows31[:], dr["conv_dw_w"].rearrange("a t (c p) -> (a t c) p", p=P)),
                                 (rows5[:], dr["gdn_conv_w"].rearrange("a t (c p) -> (a t c) p", p=P)),
                                 (small[0:1, 0:8], dr["gdn_a_log"].rearrange("a b c -> a (b c)")),
                                 (small[0:1, 8:16], dr["gdn_dt_bias"].rearrange("a b c -> a (b c)")),
                                 (small[0:1, 16:32], dr["router_bias"].rearrange("(a n) -> a n", a=1)),
                                 (small[0:1, 32:288], dr["lam_p"].rearrange("a b c -> a (b c)"))):
                    sp.dma_start(dst, src).then_inc(s("small_loaded"), 16)
                    n_small += 16
                assert n_small == PREP_SMALL
                for j in range(12):
                    if j < 10:
                        if j >= 2:
                            sp.wait_ge(s("x_normed"), j - 1)
                            sp.wait_ge(s("squared"), j - 1)
                        src = dr["ctx"][0, j * P:(j + 1) * P, :] if j < 2 else dr["x"][0, (j - 2) * P:(j - 1) * P, :]
                        sp.dma_start(xt[j % 2][:], src).then_inc(s("x_loaded", j % 2), 16)
                    if j >= 3:
                        sp.wait_ge(s("w_mod_used"), j - 2)
                    sp.dma_start(wm[j % 3], dr["w_mod"][0, :, j * 512:(j + 1) * 512]
                                 .rearrange("(c p) n -> p c n", p=P)).then_inc(s("w_mod_loaded", j % 3), 16)

            @block.tensor
            def _(pe):
                pe.wait_ge(s("small_loaded"), PREP_SMALL)
                pe.wait_ge(s("consts_loaded"), 16)
                nc.tensor.transpose(p_vec[:, 0:VEC_N], rows[:, :], k.c("ident")[0:VEC_N, 0:VEC_N])
                nc.tensor.transpose(p_vec[:, 128:252], rows31[:, :], k.c("ident")[0:124, 0:124])
                nc.tensor.transpose(p_vec[:, 256:316], rows5[:, :], k.c("ident")[0:60, 0:60]).then_inc(s("vec_turned"), 1)
                cs = silu_c[:, :].rearrange("p (m c) -> p c m", m=2)

                def turn(t):
                    pe.wait_ge(s("x_normed"), t + 1)
                    if t >= 2:
                        pe.wait_ge(s("h_stored"), t - 1)
                    for c in range(KD):
                        last = nc.tensor.transpose(p_x[t % 2][:, c * P:(c + 1) * P], xn[t % 2][:, c * P:(c + 1) * P],
                                                   k.c("ident"))
                    last.then_inc(s("x_turned"), 1)

                for j in range(12):
                    if j < 10:
                        turn(j)
                    if j == 0:
                        pe.wait_ge(s("silu_ready"), 1)
                        pe.wait_ge(s("vec_ready"), 1)
                    pe.wait_ge(s("w_mod_loaded", j % 3), 16 * (j // 3 + 1))
                    if j >= 2:
                        pe.wait_ge(s("mod_row"), j - 1)
                    for c in range(KD):
                        last = nc.tensor.matmul(p_row[j % 2][0:2, :], cs[:, c, :], wm[j % 3][:, c, :],
                                                start=(c == 0), stop=(c == KD - 1))
                    last.then_inc(s("w_mod_used"), 1)
                pe.wait_ge(s("mod_row"), 12)
                pe.wait_ge(s("h_stored"), 10)
                for t in range(48):
                    last = nc.tensor.transpose(p_mod[:, 2 * t:2 * t + 2], mod_row[0:2, t * P:(t + 1) * P],
                                               k.c("ident")[0:2, 0:2])
                last.then_inc(s("mod_turned"), 1)
                pe.wait_ge(s("rows_ready"), 1)
                nc.tensor.matmul(p_vec[:, 0:33], k.c("ones")[0:1, :], spread[0:1, :], start=True, stop=True) \
                    .then_inc(s("rows_spread"), 1)
                pe.wait_ge(s("mod_ready"), 1)
                for n, gate in enumerate((2, 5)):
                    if n:
                        pe.wait_ge(s("gate_rows_stored"), n)
                    for c in range(KD):
                        nc.tensor.matmul(p_g[:, c * P:(c + 1) * P],
                                         k.mod[:, gate * KD + c, 0:1].to_broadcast([P, P]), k.c("ident"),
                                         start=True, stop=True).then_inc(s("gate_rows"), 1)

            @block.scalar
            def _(act):
                act.wait_ge(s("vec_ready"), 1)
                nc.scalar.activation(sig_c[:, :], k.vec[:, 0:16], ACT.Sigmoid).then_inc(s("sigmoid_c"), 1)

                def store(t):
                    act.wait_ge(s("x_turned"), t + 1)
                    nc.scalar.activation(k.hT[:, :, t * P:(t + 1) * P],
                                         p_x[t % 2][:, :].rearrange("p (c n) -> p c n", c=KD), ACT.Copy) \
                        .then_inc(s("h_stored"), 1)

                def store_mod(j):
                    act.wait_ge(s("w_mod_used"), j + 1)
                    nc.scalar.activation(mod_row[0:2, j * 512:(j + 1) * 512], p_row[j % 2][0:2, :], ACT.Copy) \
                        .then_inc(s("mod_row"), 1)

                for t in range(10):
                    act.wait_ge(s("x_loaded", t % 2), 16 * (t // 2 + 1))
                    if t:
                        act.wait_ge(s("squared"), t)
                    nc.scalar.activation(sq[:, :], xt[t % 2][:], ACT.Square, accum_out=ssum[:, t:t + 1]) \
                        .then_inc(s("squared"), 1)
                    act.wait_ge(s("squared"), t + 1)
                    act.wait_ge(s("eps_set"), 1)
                    nc.scalar.activation(root[:, t:t + 1], ssum[:, t:t + 1], ACT.Sqrt, bias=k.eps[:, 0:1],
                                         scale=1.0 / D).then_inc(s("root"), 1)
                    if t:
                        store(t - 1)
                        store_mod(t - 1)
                store(9)
                act.wait_ge(s("lam_sums"), 1)
                nc.scalar.activation(lams[0:1, 2:4], lams[0:1, 0:2], ACT.Exp).then_inc(s("lam_exps"), 1)
                for j in range(9, 12):
                    store_mod(j)
                act.wait_ge(s("h_stored"), 10)
                act.wait_ge(s("mod_scaled"), 1)
                for c in range(BY_ACT):
                    nc.scalar.activation(k.hT[:, c, CTX:TOK], k.hT[:, c, CTX:TOK], ACT.Identity,
                                         bias=k.mod[:, c, 0:1], scale=k.a1[:, c, 0:1]).then_inc(s("modulated"), 1)
                for n, dst in enumerate((k.g1b, k.g2b)):
                    act.wait_ge(s("gate_rows"), KD * (n + 1))
                    nc.scalar.activation(dst[:, :], p_g[:, :], ACT.Copy).then_inc(s("gate_rows_stored"), 1)

            @block.vector
            def _(dve):
                ch = Chain(dve, s("dve_steps"))
                nc.vector.memset(k.eps[:, 0:1], EPS).then_inc(s("eps_set"), 1)
                ch.run(nc.vector.memset(k.eps[:, 1:2], 1e-5))
                dve.wait_ge(s("vec_turned"), 1)
                ch.run(nc.vector.tensor_copy(k.taps31[:, :], p_vec[:, 128:252]))
                ch.run(nc.vector.tensor_copy(k.taps5[:, :], p_vec[:, 256:316]))
                nc.vector.tensor_copy(k.vec[:, :], p_vec[:, 0:VEC_N]).then_inc(s("vec_ready"), 1)
                dve.wait_ge(s("vec_ready"), 1)
                dve.wait_ge(s("sigmoid_c"), 1)
                nc.vector.tensor_tensor(silu_c[:, :], sig_c[:, :], k.vec[:, 0:16], ALU.mult).then_inc(s("silu_ready"), 1)
                for t in range(10):
                    dve.wait_ge(s("root"), t + 1)
                    ch.run(nc.vector.reciprocal(rstd[:, t:t + 1], root[:, t:t + 1]))
                    if t >= 2:
                        dve.wait_ge(s("x_turned"), t - 1)
                    nc.vector.tensor_scalar(xn[t % 2][:], xt[t % 2][:], rstd[:, t:t + 1], None, ALU.mult) \
                        .then_inc(s("x_normed"), 1)
                sv = small[0:1, 32:288].rearrange("a (g h n) -> a g h n", g=2, h=2)
                ch.run(nc.vector.tensor_tensor(lamp[0:1, :].rearrange("a (g n) -> a g n", g=2), sv[:, :, 0, :],
                                               sv[:, :, 1, :], ALU.mult))
                nc.vector.tensor_reduce(lams[0:1, 0:2], lamp[0:1, :].rearrange("a (g n) -> a g n", g=2), AX.X, ALU.add) \
                    .then_inc(s("lam_sums"), 1)
                ch.run(nc.vector.tensor_copy(spread[0:1, 0:32], small[0:1, 0:32]))
                dve.wait_ge(s("lam_exps"), 1)
                ch.run(nc.vector.tensor_tensor(lams[0:1, 0:1], lams[0:1, 2:3], lams[0:1, 3:4], ALU.subtract))
                nc.vector.tensor_scalar(spread[0:1, 32:33], lams[0:1, 0:1], -1.0, -LAMBDA_INIT, ALU.mult, ALU.add) \
                    .then_inc(s("rows_ready"), 1)
                dve.wait_ge(s("mod_turned"), 1)
                nb = VEC["b_mod"][0]
                ch.run(nc.vector.tensor_tensor(k.mod[:, :, :], p_mod[:, 0:96].rearrange("p (j m) -> p j m", m=2),
                                               k.vec[:, nb:nb + 48].unsqueeze(2).to_broadcast([P, 48, 2]), ALU.add))
                for m, (n, at) in enumerate((("norm1_w", 1), ("norm2_w", 4))):
                    dst = (k.a1, k.a2)[m]
                    nw = VEC[n][0]
                    ch.run(nc.vector.scalar_tensor_tensor(dst[:, :, :], k.mod[:, at * KD:(at + 1) * KD, :], 1.0,
                                                          k.vec[:, nw:nw + KD].unsqueeze(2).to_broadcast([P, KD, 2]),
                                                          ALU.add, ALU.mult))
                nc.vector.tensor_copy(k.mod_done[:, 0:1], k.mod[:, 0, 0:1]).then_inc(s("mod_scaled"), 1)
                nc.vector.tensor_copy(k.mod_done[:, 1:2], k.mod[:, 0, 0:1]).then_inc(s("mod_ready"), 1)
                dve.wait_ge(s("h_stored"), 10)
                for c in range(KD):
                    nc.vector.tensor_scalar(k.hT[:, c, 0:CTX], k.hT[:, c, 0:CTX], k.a1[:, c, 1:2], k.mod[:, c, 1:2],
                                            ALU.mult, ALU.add).then_inc(s("modulated_ctx"), 1)
                for c in range(BY_ACT, KD):
                    nc.vector.tensor_scalar(k.hT[:, c, CTX:TOK], k.hT[:, c, CTX:TOK], k.a1[:, c, 0:1],
                                            k.mod[:, c, 0:1], ALU.mult, ALU.add).then_inc(s("modulated_latent"), 1)
                dve.wait_ge(s("rows_spread"), 1)
                nc.vector.tensor_copy(k.rows[:, :], p_vec[:, 0:33]).then_inc(s("rows_stored"), 1)


def w_in_tile(dr, at):
    return dr["w_in"][0, :, ds(at, P)].rearrange("(c p) n -> p c n", p=P)


def qkv(k):
    nc, dr = k.nc, k.dram
    PARTS = [(0, CTX, 512, 0), (0, CTX + 512, 512, 512), (1, CTX, 512, 0), (1, CTX + 512, 512, 512), (1, 0, CTX, None)]
    NP = len(PARTS)
    TURN = [n for n, part in enumerate(PARTS) if part[3] is not None]
    per = {"load_q": 1, "load_k": 1, "projected": NP, "squared": NP, "summed": NP, "rooted": NP, "normed": NP,
           "turned": len(TURN), "cosed": len(TURN), "sined": len(TURN), "roped": len(TURN),
           "o_squared": 2, "o_summed": 2, "o_rooted": 2, "o_normed": 2}
    with ExitStack() as st:
        s = Signals(nc, st, "qkv")
        rope = k.sb(st, "rope", [P, 2, SEQ])
        w = [k.sb(st, f"w_qk{i}", [P, KD, P]) for i in range(2)]
        wv = k.sb(st, "w_v", [P, KD, BW])
        sq = [k.sb(st, f"sq{i}", [P, 512]) for i in range(2)]
        root = [k.sb(st, f"root{i}", [P, 512]) for i in range(2)]
        rinv = k.sb(st, "rinv", [P, 512])
        qn = [k.sb(st, f"qn{i}", [P, 512]) for i in range(2)]
        t1 = [k.sb(st, f"cosed{i}", [P, 512]) for i in range(2)]
        t2 = k.sb(st, "sined", [P, 512])
        behind_v = HEADS * (SEQ + TOK) + TOK // P * BW
        o_sq = k.region[:, behind_v:behind_v + 512]
        o_root = k.region[:, behind_v + 512:behind_v + 1024]
        p_o = k.ps(st, "p_o_sum", [P, 512])

        def o_part(tensor, it, j):
            return tensor[:, ds(it, 1), 512 * j:512 * j + 512].rearrange("p a n -> p (a n)")

        p_q = [k.ps(st, f"p_q{i}", [P, 512]) for i in range(3)]
        p_s = [k.ps(st, f"p_s{i}", [P, 512]) for i in range(2)]
        p_r = [k.ps(st, f"p_r{i}", [P, 512]) for i in range(2)]

        with nc.Block() as block:
            @block.sync
            def _(sp):
                credit(s, sp, per, "load_q", "load_k")
                sp.dma_start(rope[:], dr["rope"]).then_inc(s("rope_loaded"), 16)
                with sp.Fori(0, HEADS) as it:
                    ps = Pass(s, sp, it, per)
                    src = [w_in_tile(dr, it * P + A_Q), w_in_tile(dr, it * P + A_K)]
                    ps.after_last("projected", 1)
                    sp.dma_start(w[0][:], src[0]).then_inc(s("load_q"), 16)
                    ps.after_last("projected", NP - 1)
                    sp.dma_start(w[1][:], src[1]).then_inc(s("load_k"), 16)
                sp.dma_start(wv[:], dr["w_in"][0, :, A_V:A_V + BW].rearrange("(c p) n -> p c n", p=P)) \
                    .then_inc(s("v_loaded"), 16)

            @block.tensor
            def _(pe):
                credit(s, pe, per, "projected", "summed", "turned", "o_summed")
                with pe.Fori(0, HEADS) as it:
                    ps = Pass(s, pe, it, per)

                    def project(n):
                        which, at, size, _ = PARTS[n]
                        if n in (0, 2):
                            ps.after("load_k" if which else "load_q")
                        if n < 3:
                            ps.after_last("normed", {0: 3, 1: 4, 2: 2}[n])
                        else:
                            ps.after("normed", n - 3)
                        for c in range(KD):
                            last = nc.tensor.matmul(p_q[n % 3][:, 0:size], w[which][:, c, :], k.hT[:, c, at:at + size],
                                                    start=(c == 0), stop=(c == KD - 1))
                        last.then_inc(s("projected"), 1)

                    def sum_squares(n):
                        size = PARTS[n][2]
                        ps.after("squared", n)
                        if n < 2:
                            ps.after_last("rooted", 4 if n == 0 else 3)
                        else:
                            ps.after("rooted", n - 2)
                        nc.tensor.matmul(p_s[n % 2][:, 0:size], k.c("blk"), sq[n % 2][:, 0:size], start=True,
                                         stop=True).then_inc(s("summed"), 1)

                    def turn(r):
                        ps.after("normed", TURN[r])
                        if r < 2:
                            ps.after_last("sined", r + 2)
                        else:
                            ps.after("sined", r - 2)
                        nc.tensor.matmul(p_r[r % 2][:, :], k.c("rot"), qn[TURN[r] % 2][:, :], start=True, stop=True) \
                            .then_inc(s("turned"), 1)

                    def sum_outputs(j):
                        ps.after("o_squared", j)
                        ps.after("o_rooted", 0) if j else ps.after_last("o_rooted", 1)
                        nc.tensor.matmul(p_o[:, :], k.c("ones"), o_sq, start=True, stop=True) \
                            .then_inc(s("o_summed"), 1)

                    project(0)
                    sum_outputs(0)
                    project(1)
                    sum_squares(0)
                    project(2)
                    sum_squares(1)
                    turn(0)
                    project(3)
                    sum_squares(2)
                    turn(1)
                    sum_outputs(1)
                    project(4)
                    sum_squares(3)
                    turn(2)
                    sum_squares(4)
                    turn(3)
                pe.wait_ge(s("v_loaded"), 16)
                for t in range(TOK // P):
                    if t >= 2:
                        pe.wait_ge(s("v_stored"), t - 1)
                    if t == 0:
                        pe.wait_ge(s("normed"), NP * (HEADS + 1))
                    for c in range(KD):
                        last = nc.tensor.matmul(p_q[t % 2][:, :], k.hT[:, c, t * P:(t + 1) * P], wv[:, c, :],
                                                start=(c == 0), stop=(c == KD - 1))
                    last.then_inc(s("v_projected"), 1)

            @block.scalar
            def _(act):
                credit(s, act, per, "squared", "rooted", "o_squared", "o_rooted")
                with act.Fori(0, HEADS) as it:
                    ps = Pass(s, act, it, per)

                    def square(n):
                        size = PARTS[n][2]
                        ps.after("projected", n)
                        if n < 2:
                            ps.after_last("summed", 4 if n == 0 else 3)
                        else:
                            ps.after("summed", n - 2)
                        nc.scalar.activation(sq[n % 2][:, 0:size], p_q[n % 3][:, 0:size], ACT.Square) \
                            .then_inc(s("squared"), 1)

                    def take_root(n):
                        size = PARTS[n][2]
                        ps.after("summed", n)
                        if n < 2:
                            ps.after_last("normed", 4 if n == 0 else 3)
                        else:
                            ps.after("normed", n - 2)
                        nc.scalar.activation(root[n % 2][:, 0:size], p_s[n % 2][:, 0:size], ACT.Sqrt,
                                             bias=k.eps[:, 0:1], scale=1.0 / 64).then_inc(s("rooted"), 1)

                    def square_outputs(j):
                        ps.after("o_summed", 0) if j else ps.after_last("o_summed", 1)
                        nc.scalar.activation(o_sq, o_part(k.oT, it, j), ACT.Square).then_inc(s("o_squared"), 1)

                    def root_outputs(j):
                        ps.after("o_summed", j)
                        ps.after("o_normed", 0) if j else ps.after_last("o_normed", 1)
                        nc.scalar.activation(o_root, p_o[:, :], ACT.Sqrt, bias=k.eps[:, 0:1], scale=1.0 / P) \
                            .then_inc(s("o_rooted"), 1)

                    square_outputs(0)
                    square(0)
                    for n in range(NP):
                        if n + 1 < NP:
                            square(n + 1)
                        take_root(n)
                        if n == 0:
                            root_outputs(0)
                            square_outputs(1)
                        elif n == 2:
                            root_outputs(1)
                for t in range(TOK // P):
                    act.wait_ge(s("v_projected"), t + 1)
                    nc.scalar.activation(k.v[:, t, :], p_q[t % 2][:, :], ACT.Copy).then_inc(s("v_stored"), 1)

            @block.gpsimd
            def _(pool):
                credit(s, pool, per, "cosed")
                pool.wait_ge(s("rope_loaded"), 16)
                with pool.Fori(0, HEADS) as it:
                    ps = Pass(s, pool, it, per)
                    for r, n in enumerate(TURN):
                        pos = PARTS[n][3]
                        ps.after("normed", n)
                        if r < 2:
                            ps.after_last("roped", r + 2)
                        else:
                            ps.after("roped", r - 2)
                        nc.gpsimd.tensor_tensor(t1[r % 2][:, :], qn[n % 2][:, :], rope[:, 0, pos:pos + 512], ALU.mult) \
                            .then_inc(s("cosed"), 1)
                        if r % 2:
                            j = r // 2
                            ps.after("o_normed", j)
                            nc.gpsimd.tensor_tensor(o_part(k.oT, it, j), o_part(k.oT, it, j), o_part(k.zT, it, j),
                                                    ALU.mult).then_inc(s("o_gated"), 1)

            @block.vector
            def _(dve):
                ch = Chain(dve, s("dve_steps"))
                credit(s, dve, per, "normed", "sined", "roped", "o_normed")
                dve.wait_ge(s("rope_loaded"), 16)
                with dve.Fori(0, HEADS) as it:
                    ch.enter(it, NP + 2)
                    ps = Pass(s, dve, it, per)

                    def norm(n):
                        which, at, size, pos = PARTS[n]
                        ps.after("rooted", n)
                        if n:
                            ps.after("normed", n - 1)
                        else:
                            ps.after_last("normed")
                        ch.run(nc.vector.reciprocal(rinv[:, 0:size], root[n % 2][:, 0:size]))
                        if pos is None:
                            dst = k.kT[:, ds(it, 1), 0:size].rearrange("p a n -> p (a n)")
                        else:
                            dst = qn[n % 2][:, :]
                            r = TURN.index(n)
                            r0 = {0: (1, 2), 1: (1, 3), 2: (0, 0), 3: (0, 1)}[r]
                            if r0[0]:
                                ps.after_last("turned", r0[1])
                                ps.after_last("cosed", r0[1])
                            else:
                                ps.after("turned", r0[1])
                                ps.after("cosed", r0[1])
                        wc = k.col("kn_w" if which else "qn_w")
                        nc.vector.scalar_tensor_tensor(dst, p_q[n % 3][:, 0:size], wc, rinv[:, 0:size], ALU.mult,
                                                       ALU.mult).then_inc(s("normed"), 1)

                    def rotate(r):
                        which, at, size, pos = PARTS[TURN[r]]
                        ps.after("turned", r)
                        if r:
                            ps.after("roped", r - 1)
                        else:
                            ps.after_last("roped")
                        nc.vector.tensor_tensor(t2[:, :], p_r[r % 2][:, :], rope[:, 1, pos:pos + 512], ALU.mult) \
                            .then_inc(s("sined"), 1)
                        ps.after("sined", r)
                        ps.after("cosed", r)
                        full, off = (k.kT, CTX) if which else (k.qT, 0)
                        nc.vector.tensor_tensor(full[:, ds(it, 1), off + pos:off + pos + 512]
                                                .rearrange("p a n -> p (a n)"), t1[r % 2][:, :], t2[:, :], ALU.add) \
                            .then_inc(s("roped"), 1)

                    def norm_outputs(j):
                        ps.after("o_rooted", j)
                        ch.run(nc.vector.reciprocal(o_root, o_root))
                        nc.vector.scalar_tensor_tensor(o_part(k.oT, it, j), o_part(k.oT, it, j), k.col("gdn_norm_w"),
                                                       o_root, ALU.mult, ALU.mult).then_inc(s("o_normed"), 1)

                    norm(0)
                    norm(1)
                    norm_outputs(0)
                    rotate(0)
                    norm(2)
                    rotate(1)
                    norm(3)
                    rotate(2)
                    norm(4)
                    rotate(3)
                    norm_outputs(1)
                ch.leave(HEADS)


def attend(k):
    nc, dr = k.nc, k.dram
    NQ = SEQ // P
    NKT = TOK // P
    GROUPS = [(0, 4), (4, 4), (8, 2)]
    SCALE = 64 ** -0.5
    per = {"staged": 2, "scored": 8, "maxed": 8, "exped": 8, "mixed": 4, "turned": 12, "stored": 12, "attended": 4,
           "saved": 4, "rooted": 1, "normed": 1, "y_turned": 1, "y_stored": 1}
    with ExitStack() as st:
        s = Signals(nc, st, "att")
        qb = k.sb(st, "q_block", [P, 2, HEADS, P])
        pm = [[k.sb(st, f"p{m}{i}", [P, TOK]) for m in range(2)] for i in range(2)]
        aT = [k.sb(st, f"aT{i}", [P, NKT * P]) for i in range(2)]
        top = k.sb(st, "row_max", [P, 8])
        nb = k.sb(st, "minus_max", [P, 8])
        total = k.sb(st, "exp_sum", [P, 8])
        inv = k.sb(st, "inverse_sum", [P, 8])
        o_raw = k.sb(st, "o_raw", [P, HEADS, P])
        o_n = k.sb(st, "o_normed", [P, HEADS, P])
        osq = k.sb(st, "o_squares", [P, P])
        ssum = k.sb(st, "o_square_sum", [P, HEADS])
        root = k.sb(st, "o_root", [P, HEADS])
        rinv = k.sb(st, "o_inverse", [P, HEADS])
        subw = k.sb(st, "subln_scaled", [P, 1])
        p_s = [k.ps(st, f"p_scores{m}", [P, 1536]) for m in range(2)]
        p_t = [k.ps(st, f"p_turned{i}", [P, 512]) for i in range(2)]

        with nc.Block() as block:
            @block.sync
            def _(sp):
                for w, at, name in ((k.w_b[0], B_A, "load_a"), (k.w_b[1], B_A + BW, "load_g")):
                    sp.dma_start(w[:], w_in_tile(dr, at)).then_inc(k.brn_signals(name), 16)

            @block.gpsimd
            def _(pool):
                credit(s, pool, per, "staged")
                nc.gpsimd.memset(qb[64:128, 0, :, :], 0.0).then_inc(s("zeroed"), 1)
                nc.gpsimd.memset(qb[0:64, 1, :, :], 0.0).then_inc(s("zeroed"), 1)
                with pool.Fori(0, NQ) as it:
                    ps = Pass(s, pool, it, per)
                    ps.after_last("scored")
                    for m in range(2):
                        part = slice(64 * m, 64 * m + 64)
                        nc.gpsimd.tensor_copy(qb[part, m, :, :], k.qT[part, :, ds(it * P, P)]).then_inc(s("staged"), 1)

            @block.tensor
            def _(pe):
                credit(s, pe, per, "scored", "turned", "attended", "y_turned")
                pe.wait_ge(s("zeroed"), 2)

                def turn_outputs(ps):
                    ps.after("normed")
                    for h in range(HEADS):
                        last = nc.tensor.transpose(p_t[0][:, h * P:(h + 1) * P], o_n[:, h, :], k.c("ident"))
                    last.then_inc(s("y_turned"), 1)

                def queries(ps, first_pass, last_pass):
                    def scores(ps, h):
                        if h == 0:
                            ps.after("staged")
                        for m in range(2):
                            n = 2 * h + m
                            if h == 0:
                                ps.after_last("exped", 6 + m)
                            else:
                                ps.after("exped", n - 2)
                            for at, size in ((0, 512), (512, 512), (1024, 256)):
                                last = nc.tensor.matmul(p_s[m][:, at:at + size], qb[:, m, h, :],
                                                        k.kT[:, h, at:at + size], start=True, stop=True)
                            last.then_inc(s("scored"), 1)

                    def turn(h):
                        ps.after("mixed", h)
                        for g, (at, size) in enumerate(GROUPS):
                            if g == 0:
                                ps.after_last("y_stored") if h == 0 else ps.after("stored", 3 * h - 1)
                            elif g == 1:
                                ps.after_last("saved") if h == 0 else ps.after("saved", h - 1)
                            else:
                                ps.after("stored", 3 * h)
                            for t in range(size):
                                last = nc.tensor.transpose(p_t[g % 2][:, t * P:(t + 1) * P],
                                                           pm[h % 2][0][:, (at + t) * P:(at + t + 1) * P],
                                                           k.c("ident"))
                            last.then_inc(s("turned"), 1)

                    def weigh(h):
                        ps.after("stored", 3 * h + 2)
                        for t in range(NKT):
                            last = nc.tensor.matmul(p_t[1][:, 0:P], aT[h % 2][:, t * P:(t + 1) * P],
                                                    k.v[:, t, h * P:(h + 1) * P], start=(t == 0), stop=(t == NKT - 1))
                        last.then_inc(s("attended"), 1)

                    if ps is None:
                        scores(Pass(s, pe, 0, per), 0)
                        return
                    for h in range(HEADS):
                        if h + 1 < HEADS:
                            scores(ps, h + 1)
                        elif not last_pass:
                            scores(ps.step(-1), 0)
                        if h == 0 and not first_pass:
                            turn_outputs(ps.step(1))
                        turn(h)
                        weigh(h)

                queries(None, True, False)
                queries(Pass(s, pe, 0, per), True, False)
                with pe.Fori(1, NQ - 1) as it:
                    queries(Pass(s, pe, it, per), False, False)
                queries(Pass(s, pe, NQ - 1, per), False, True)
                turn_outputs(Pass(s, pe, NQ - 1, per))

            @block.scalar
            def _(act):
                credit(s, act, per, "exped", "stored", "saved", "rooted", "y_stored")
                act.wait_ge(s("subln_scaled"), 1)

                def store_outputs(ps, it):
                    ps.after("y_turned")
                    nc.scalar.activation(k.yaT[:, :, ds(it * P, P)], p_t[0][:, :].rearrange("p (h n) -> p h n", h=4),
                                         ACT.Copy, scale=subw[:, 0:1]).then_inc(s("y_stored"), 1)

                def queries(ps, it, first_pass, last_pass):
                    def exps(ps, h):
                        for m in range(2):
                            n = 2 * h + m
                            ps.after("maxed", n)
                            if h < 2:
                                ps.after_last("turned", 3 * (h + 2) + 2)
                            else:
                                ps.after("turned", 3 * (h - 2) + 2)
                            nc.scalar.activation(pm[h % 2][m][:, :], p_s[m][:, 0:TOK], ACT.Exp, bias=nb[:, n:n + 1],
                                                 scale=SCALE, accum_out=total[:, n:n + 1]).then_inc(s("exped"), 1)

                    if ps is None:
                        exps(Pass(s, act, 0, per), 0)
                        return
                    if not first_pass:
                        store_outputs(ps.step(1), it - 1)
                    for h in range(HEADS):
                        for g, (at, size) in enumerate(GROUPS):
                            ps.after("turned", 3 * h + g)
                            if g == 0:
                                ps.after_last("attended", h + 2) if h < 2 else ps.after("attended", h - 2)
                            nc.scalar.activation(aT[h % 2][:, at * P:(at + size) * P], p_t[g % 2][:, 0:size * P],
                                                 ACT.Copy).then_inc(s("stored"), 1)
                        if h + 1 < HEADS:
                            exps(ps, h + 1)
                        elif not last_pass:
                            exps(ps.step(-1), 0)
                        ps.after("attended", h)
                        if h == 0:
                            ps.after_last("normed")
                            ps.after_last("saved")
                        else:
                            ps.after("saved", h - 1)
                        nc.scalar.activation(osq[:, :], p_t[1][:, 0:P], ACT.Square, accum_out=ssum[:, h:h + 1])
                        nc.scalar.activation(o_raw[:, h, :], p_t[1][:, 0:P], ACT.Copy).then_inc(s("saved"), 1)
                    ps.after("saved")
                    nc.scalar.activation(root[:, :], ssum[:, :], ACT.Sqrt, bias=k.eps[:, 1:2], scale=1.0 / P) \
                        .then_inc(s("rooted"), 1)

                queries(None, None, True, False)
                queries(Pass(s, act, 0, per), 0, True, False)
                with act.Fori(1, NQ - 1) as it:
                    queries(Pass(s, act, it, per), it, False, False)
                queries(Pass(s, act, NQ - 1, per), NQ - 1, False, True)
                store_outputs(Pass(s, act, NQ - 1, per), NQ - 1)

            @block.vector
            def _(dve):
                ch = Chain(dve, s("dve_steps"))
                credit(s, dve, per, "maxed", "mixed", "normed")
                nc.vector.tensor_scalar(subw[:, :], k.col("subln_w"), 1.0 - LAMBDA_INIT, None, ALU.mult) \
                    .then_inc(s("subln_scaled"), 1)

                def queries(ps, last_pass):
                    def maxima(ps, h):
                        for m in range(2):
                            n = 2 * h + m
                            ps.after("scored", n)
                            ps.after_last("exped", n)
                            ch.run(nc.vector.tensor_reduce(top[:, n:n + 1], p_s[m][:, 0:TOK], AX.X, ALU.max))
                            nc.vector.tensor_scalar(nb[:, n:n + 1], top[:, n:n + 1], -SCALE, None, ALU.mult) \
                                .then_inc(s("maxed"), 1)

                    def mix(h):
                        a, b = pm[h % 2]
                        n = 2 * h
                        ps.after("exped", n + 1)
                        ch.run(nc.vector.reciprocal(inv[:, n:n + 2], total[:, n:n + 2]))
                        ch.run(nc.vector.tensor_tensor(inv[:, n + 1:n + 2], inv[:, n + 1:n + 2], k.rows[:, 32:33],
                                                       ALU.mult))
                        ch.run(nc.vector.tensor_scalar(a[:, :], a[:, :], inv[:, n:n + 1], None, ALU.mult))
                        nc.vector.scalar_tensor_tensor(a[:, :], b[:, :], inv[:, n + 1:n + 2], a[:, :], ALU.mult,
                                                       ALU.add).then_inc(s("mixed"), 1)

                    if ps is None:
                        maxima(Pass(s, dve, 0, per), 0)
                        return
                    for h in range(HEADS):
                        mix(h)
                        if h + 1 < HEADS:
                            maxima(ps, h + 1)
                        elif not last_pass:
                            maxima(ps.step(-1), 0)
                    ps.after("rooted")
                    ps.after_last("y_turned")
                    ch.run(nc.vector.reciprocal(rinv[:, :], root[:, :]))
                    nc.vector.tensor_tensor(o_n[:, :, :], o_raw[:, :, :], rinv[:, :].unsqueeze(2)
                                            .to_broadcast([P, HEADS, P]), ALU.mult).then_inc(s("normed"), 1)

                queries(None, False)
                with dve.Fori(0, NQ - 1) as it:
                    ch.enter(it, 8 + 3 * HEADS + 1)
                    queries(Pass(s, dve, it, per), False)
                ch.leave(NQ - 1)
                queries(Pass(s, dve, NQ - 1, per), True)


def delta_in(k):
    nc, dr = k.nc, k.dram
    CHUNKS = [(0, CTX, 2), (CTX, 512, 262), (CTX + 512, 512, 774)]
    SPANS = [(0, 428), (428, 428), (856, 428)]
    BANK_LAST = {0: 8, 1: 9, 2: 10, 3: 7}
    per = {"load_w0": 1, "load_w1": 1, "load_w2": 1, "load_w3": 1, "projected": 11, "raw": 9, "z_sigmoid": 2,
           "z_done": 2, "convolved": 3, "sigmoid": 3, "silu": 3, "squared": 2, "summed": 2, "rooted": 2, "scaled": 2}
    with ExitStack() as st:
        s = Signals(nc, st, "din")
        w = [k.sb(st, f"w_c{i}", [P, KD, P]) for i in range(4)]
        w16 = k.sb(st, "w_beta", [P, KD, 16])
        raw = [k.sb(st, f"raw{i}", [P, RAW]) for i in range(2)]
        k.zsig = k.sb(st, "z_sigmoid", [P, 2, 512])
        k.head_taps = k.sb(st, "head_taps", [P, 15])
        acc = [k.sb(st, f"conv{i}", [P, CW]) for i in range(2)]
        sig = k.sb(st, "sig", [P, CW])
        spare = k.oT[:, :, :].rearrange("p a n -> p (a n)")
        sq = [k.sb(st, "sq", [P, CW]), spare[:, 0:CW]]
        root = [spare[:, CW:2 * CW], spare[:, 2 * CW:3 * CW]]
        bT = spare[:, CW:CW + TOK]
        za = k.sb(st, "decay_in", [P, 10, 8])
        zb = k.sb(st, "decay_min", [P, 10, 8])
        ea = k.sb(st, "exp_a_log", [P, 8])
        p_w = [k.ps(st, f"p_w{i}", [P, 512]) for i in range(4)]
        p_s = k.ps(st, "p_sum", [P, 1536])
        p_b = k.ps(st, "p_beta", [P, 512])

        def before(ps, name, n):
            if n == 2:
                ps.after(name, 0)
            else:
                ps.after_last(name, 2 - n)

        with nc.Block() as block:
            @block.sync
            def _(sp):
                credit(s, sp, per, "load_w0", "load_w1", "load_w2", "load_w3")
                sp.dma_start(w16[:], dr["w_in"][0, :, C_BETA:C_BETA + 16].rearrange("(c p) n -> p c n", p=P)) \
                    .then_inc(s("beta_loaded"), 16)
                with sp.Fori(0, HEADS) as it:
                    ps = Pass(s, sp, it, per)
                    src = [w_in_tile(dr, it * P + C_Q + BW * n) for n in range(4)]
                    for n, last in enumerate((2, 5, 8, 10)):
                        ps.after_last("projected", last)
                        sp.dma_start(w[n][:], src[n]).then_inc(s(f"load_w{n}"), 16)

            @block.tensor
            def _(pe):
                credit(s, pe, per, "projected", "summed")
                with pe.Fori(0, HEADS) as it:
                    ps = Pass(s, pe, it, per)

                    def project(n, chunks):
                        ps.after(f"load_w{n}")
                        for at, size, _ in chunks:
                            i = 3 * n + (CHUNKS if n < 3 else CHUNKS[1:]).index((at, size, _))
                            if i < 4:
                                prev, wait = BANK_LAST[i], ps.after_last
                            else:
                                prev, wait = i - 4, ps.after
                            wait("z_done" if prev > 8 else "raw", prev - 9 if prev > 8 else prev)
                            for c in range(KD):
                                last = nc.tensor.matmul(p_w[i % 4][:, 0:size], w[n][:, c, :],
                                                        k.hT[:, c, at:at + size], start=(c == 0), stop=(c == KD - 1))
                            last.then_inc(s("projected"), 1)

                    def sum_squares(n):
                        ps.after("squared", n)
                        ps.after_last("rooted") if n == 0 else ps.after("rooted", 0)
                        for b, (at, size) in enumerate(SPANS):
                            last = nc.tensor.matmul(p_s[:, 512 * b:512 * b + size], k.c("ones"), sq[n][:, at:at + size],
                                                    start=True, stop=True)
                        last.then_inc(s("summed"), 1)

                    project(0, CHUNKS)
                    project(1, CHUNKS)
                    project(2, CHUNKS)
                    sum_squares(0)
                    project(3, CHUNKS[1:])
                    sum_squares(1)
                pe.wait_ge(s("beta_loaded"), 16)
                pe.wait_ge(s("raw"), 9 * (HEADS + 1))
                pe.wait_ge(s("z_done"), 2 * (HEADS + 1))
                for i, (at, size, _) in enumerate(CHUNKS):
                    for c in range(KD):
                        last = nc.tensor.matmul(p_w[i][0:16, 0:size], w16[:, c, :], k.hT[:, c, at:at + size],
                                                start=(c == 0), stop=(c == KD - 1))
                    last.then_inc(s("beta_rows"), 1)
                for t in range(TOK // P):
                    pe.wait_ge(s("beta_rows_stored"), 1 if t < 2 else 2 if t < 6 else 3)
                    last = nc.tensor.transpose(p_b[:, 16 * t:16 * t + 16], bT[0:16, t * P:(t + 1) * P],
                                               k.c("ident")[0:16, 0:16])
                last.then_inc(s("beta_projected"), 1)

            @block.scalar
            def _(act):
                credit(s, act, per, "raw", "z_sigmoid", "sigmoid", "squared", "rooted")
                with act.Fori(0, HEADS) as it:
                    ps = Pass(s, act, it, per)

                    def store(n):
                        before(ps, "convolved", n)
                        for i, (at, size, to) in enumerate(CHUNKS):
                            ps.after("projected", 3 * n + i)
                            nc.scalar.activation(raw[n % 2][:, to:to + size], p_w[(3 * n + i) % 4][:, 0:size],
                                                 ACT.Copy).then_inc(s("raw"), 1)

                    def sigmoid(n):
                        ps.after("convolved", n)
                        ps.after("silu", n - 1) if n else ps.after_last("silu")
                        nc.scalar.activation(sig[:, :], acc[n % 2][:, :], ACT.Sigmoid).then_inc(s("sigmoid"), 1)

                    def square(n):
                        ps.after("silu", n)
                        ps.after_last("summed", n)
                        nc.scalar.activation(sq[n][:, :], k.cT[:, ds(it + 4 * n, 1), :].rearrange("p a n -> p (a n)"),
                                             ACT.Square).then_inc(s("squared"), 1)

                    def take_root(n):
                        ps.after_last("scaled", n)
                        ps.after("summed", n)
                        nc.scalar.activation(root[n][:, :].rearrange("p (b n) -> p b n", b=3),
                                             p_s[:, :].rearrange("p (b n) -> p b n", b=3)[:, :, 0:428], ACT.Sqrt,
                                             bias=k.eps[:, 0:1]).then_inc(s("rooted"), 1)

                    store(0)
                    store(1)
                    sigmoid(0)
                    store(2)
                    square(0)
                    sigmoid(1)
                    take_root(0)
                    square(1)
                    for i in range(2):
                        ps.after("projected", 9 + i)
                        ps.after_last("z_done", i)
                        nc.scalar.activation(k.zsig[:, i, :], p_w[(9 + i) % 4][:, :], ACT.Sigmoid) \
                            .then_inc(s("z_sigmoid"), 1)
                    sigmoid(2)
                    take_root(1)
                act.wait_ge(s("scaled"), 2 * (HEADS + 1))
                for i, (at, size, _) in enumerate(CHUNKS):
                    act.wait_ge(s("beta_rows"), i + 1)
                    nc.scalar.activation(bT[0:16, at:at + size], p_w[i][0:16, 0:size], ACT.Copy) \
                        .then_inc(s("beta_rows_stored"), 1)
                act.wait_ge(s("beta_projected"), 1)
                nc.scalar.activation(k.beta[:, :, :], p_b[:, 0:160].rearrange("p (t n) -> p t n", t=10)[:, :, 0:8],
                                     ACT.Sigmoid).then_inc(s("beta_done"), 1)
                act.wait_ge(s("decay_in"), 1)
                nc.scalar.activation(zb[:, :, :], zb[:, :, :], ACT.Exp).then_inc(s("decay_exp"), 1)
                nc.scalar.activation(ea[:, :], k.rows[:, 0:8], ACT.Exp).then_inc(s("decay_exp"), 1)
                act.wait_ge(s("decay_exp"), 2)
                nc.scalar.activation(zb[:, :, :], zb[:, :, :], ACT.Ln, bias=1.0).then_inc(s("decay_ln"), 1)

            @block.gpsimd
            def _(pool):
                credit(s, pool, per, "silu")
                for i in range(2):
                    for at, n in ((0, 2), (258, 4), (RAW - 2, 2)):
                        nc.gpsimd.memset(raw[i][:, at:at + n], 0.0).then_inc(s("padded"), 1)
                with pool.Fori(0, HEADS) as it:
                    ps = Pass(s, pool, it, per)
                    for n in range(3):
                        ps.after("sigmoid", n)
                        nc.gpsimd.tensor_tensor(k.cT[:, ds(it + 4 * n, 1), :].rearrange("p a n -> p (a n)"),
                                                acc[n % 2][:, :], sig[:, :], ALU.mult).then_inc(s("silu"), 1)

            @block.vector
            def _(dve):
                ch = Chain(dve, s("dve_steps"))
                credit(s, dve, per, "z_done", "convolved", "scaled")
                dve.wait_ge(s("padded"), 6)
                with dve.Fori(0, HEADS) as it:
                    ch.enter(it, 1 + 3 * 4 + 2)
                    ps = Pass(s, dve, it, per)

                    def taps(n):
                        return k.head_taps[:, 5 * n:5 * n + 5]

                    before(ps, "convolved", 0)
                    ch.run(nc.vector.tensor_copy(k.head_taps[:, :].rearrange("p (n t) -> p n t", n=3),
                                                 k.taps5[:, :].rearrange("p (t n h) -> p n t h", t=5, n=3)
                                                 [:, :, :, ds(it, 1)].rearrange("p n t a -> p n (t a)")))

                    def convolve(n):
                        ps.after("raw", 3 * n + 2)
                        before(ps, "silu", n)
                        src, dst = raw[n % 2], acc[n % 2]
                        ch.run(nc.vector.tensor_scalar(dst[:, :], src[:, 0:CW], taps(n)[:, 0:1], None, ALU.mult))
                        for t in range(1, 5):
                            ins = nc.vector.scalar_tensor_tensor(dst[:, :], src[:, t:t + CW], taps(n)[:, t:t + 1],
                                                                 dst[:, :], ALU.mult, ALU.add)
                            if t < 4:
                                ch.run(ins)
                            else:
                                ins.then_inc(s("convolved"), 1)

                    def scale(n):
                        ps.after("rooted", n)
                        r = root[n]
                        ch.run(nc.vector.reciprocal(r[:, :], r[:, :]))
                        y = k.cT[:, ds(it + 4 * n, 1), :].rearrange("p a n -> p (a n)")
                        nc.vector.scalar_tensor_tensor(y, y, (P ** -0.5, 1.0)[n], r[:, :], ALU.mult, ALU.mult) \
                            .then_inc(s("scaled"), 1)

                    convolve(0)
                    convolve(1)
                    convolve(2)
                    scale(0)
                    for i in range(2):
                        ps.after("z_sigmoid", i)
                        nc.vector.tensor_tensor(k.zT[:, ds(it, 1), 512 * i:512 * i + 512]
                                                .rearrange("p a n -> p (a n)"), p_w[(9 + i) % 4][:, :],
                                                k.zsig[:, i, :], ALU.mult).then_inc(s("z_done"), 1)
                    scale(1)
                ch.leave(HEADS)
                dve.wait_ge(s("beta_projected"), 1)
                dve.wait_ge(s("beta_done"), 1)
                ch.run(nc.vector.tensor_tensor(za[:, :, :], p_b[:, 0:160].rearrange("p (t n) -> p t n", t=10)[:, :, 8:16],
                                               k.rows[:, 8:16].unsqueeze(1).to_broadcast([P, 10, 8]), ALU.add))
                nc.vector.scalar_tensor_tensor(zb[:, :, :], za[:, :, :], -1.0, za[:, :, :], ALU.mult, ALU.min).then_inc(s("decay_in"), 1)
                ch.run(nc.vector.tensor_scalar(za[:, :, :], za[:, :, :], 0.0, None, ALU.max))
                dve.wait_ge(s("decay_ln"), 1)
                ch.run(nc.vector.tensor_tensor(za[:, :, :], za[:, :, :], zb[:, :, :], ALU.add))
                ch.run(nc.vector.tensor_scalar(za[:, :, :], za[:, :, :], -1.0, None, ALU.mult))
                ch.run(nc.vector.tensor_tensor(k.g[:, :, :], za[:, :, :], ea[:, :].unsqueeze(1)
                                               .to_broadcast([P, 10, 8]), ALU.mult))


def delta(k):
    nc = k.nc
    NCH, NPRE = TOK // P, CTX // P
    NL = len(LEVELS)
    per = {"staged": 2, "kv_turned": 2, "cum": 2, "cum_read": 2, "neg": 2, "beta_rows": 2, "exp_rows": 2,
           "exp_cols": 2, "kv_scaled": 2, "kk": 2, "decayed": 2, "lt": 2, "at": 2, "masked": 2 * NL, "dt": 2 * NL,
           "d2": 2, "d": 2 * (NL - 2), "x": 2 * NL, "x_stored": 2 * (NL - 1), "dx": 2 * (NL - 2), "dxt": 2 * (NL - 1), "w": 2,
           "w_stored": 2, "v": 2, "v_stored": 2, "q_decayed": 2, "s_decayed": 2, "o": 2, "o_added": 2, "ds": 2,
           "s_done": 2}

    with ExitStack() as st:
        s = Signals(nc, st, "del")

        def tiles(name):
            return [k.sb(st, f"{name}{d}", [P, HEADS, P]) for d in range(2)]

        kTs, vTs, kd, kbg, vb = (tiles(n) for n in ("kT_chunk", "vT_chunk", "k_to_end", "k_beta_exp", "v_beta"))
        at_, eg, lt, lm, dm, dt, S = (tiles(n) for n in ("decay", "exp_row", "lt", "masked", "d", "dt", "state"))
        xs, wT, vn, sd = vTs, lm, lt, dm
        gb = [k.sb(st, f"g_beta{d}", [P, 8]) for d in range(2)]
        sc = [k.sb(st, f"scalars{d}", [P, 28]) for d in range(2)]
        pa, pb, pc, pd = ([k.ps(st, f"p_{n}{d}", [P, 512]) for d in range(2)] for n in "abcd")

        def heads(ap):
            return ap.rearrange("p (h n) -> p h n", h=HEADS)

        def wide(col):
            return col.unsqueeze(2).to_broadcast([P, HEADS, P])

        GC, NGC, TOEND, KDS, EXC, BEG, EGL = range(0, 28, 4)

        def passes(eng, body):
            with eng.Fori(0, NPRE) as it:
                tile = [it, it * -1 + (NPRE - 1)]
                body(it, tile, [t * P for t in tile], False)
            with eng.Fori(NPRE, NCH) as it:
                tile = [it, it * -1 + (NCH - 1 + NPRE)]
                body(it, tile, [t * P + (LAT - CTX) for t in tile], True)

        with nc.Block() as block:
            @block.gpsimd
            def _(pool):
                credit(s, pool, per, "staged", "masked", "q_decayed", "s_decayed")

                def body(it, tile, at, out):
                    ps = Pass(s, pool, it, per)
                    for d in range(2):
                        ps.after_last("kk", d)
                        ps.after_last("w", d)
                        ps.after_last("kv_scaled", d)
                        ps.after_last("exp_cols", d)
                        ps.after_last("beta_rows", d)
                        nc.gpsimd.tensor_copy(kTs[d][:, :, :], k.cT[:, HEADS:2 * HEADS, ds(at[d], P)]) \
                            .then_inc(s("stage_part"), 1)
                        ps.after_last("dxt", 2 * (NL - 2) + d)
                        nc.gpsimd.tensor_copy(vTs[d][:, :, :], k.cT[:, 2 * HEADS:3 * HEADS, ds(at[d], P)]) \
                            .then_inc(s("stage_part"), 1)
                        nc.gpsimd.tensor_copy(gb[d][:, 0:4], k.g[:, ds(tile[d], 1), 4 * d:4 * d + 4]
                                              .rearrange("p a n -> p (a n)")).then_inc(s("stage_part"), 1)
                        nc.gpsimd.tensor_copy(gb[d][:, 4:8], k.beta[:, ds(tile[d], 1), 4 * d:4 * d + 4]
                                              .rearrange("p a n -> p (a n)")).then_inc(s("staged"), 1)
                    for d in range(2):
                        ps.after("exp_rows", d)
                        ps.after("cum_read", d)
                        nc.gpsimd.tensor_tensor(eg[d][:, :, :], eg[d][:, :, :], k.cT[:, 0:HEADS, ds(at[d], P)],
                                                ALU.mult).then_inc(s("q_decayed"), 1)
                    for n in range(NL):
                        for d in range(2):
                            if n == 0:
                                ps.after("lt", d)
                                ps.after_last("v", d)
                            elif n == 1:
                                ps.after("dt", d)
                            else:
                                ps.after("x", 2 * (n - 1) + d)
                            mask = k.c(f"lev{d}", n).unsqueeze(1).to_broadcast([P, HEADS, P])
                            nc.gpsimd.tensor_tensor(lm[d][:, :, :], lt[d][:, :, :], mask, ALU.mult) \
                                .then_inc(s("masked"), 1)
                    for d in range(2):
                        ps.after("x", 2 * (NL - 1) + d)
                        ps.after_last("s_done", d)
                        nc.gpsimd.tensor_tensor(sd[d][:, :, :], S[d][:, :, :], wide(sc[d][:, EGL:EGL + 4]), ALU.mult) \
                            .then_inc(s("s_decayed"), 1)

                pool.wait_ge(s("zeroed"), 2)
                passes(pool, body)

            @block.tensor
            def _(pe):
                credit(s, pe, per, "kv_turned", "cum", "neg", "beta_rows", "kk", "x", "dx", "dxt", "w", "v", "o", "ds")
                pe.wait_ge(s("zeroed"), 2)

                def four(bank, lhs, rhs, start=True, stop=True):
                    for h in range(HEADS):
                        last = nc.tensor.matmul(bank[:, h * P:(h + 1) * P], lhs(h), rhs(h), start=start, stop=stop)
                    return last

                def body(it, tile, at, out):
                    ps = Pass(s, pe, it, per)
                    for d in range(2):
                        ps.after("staged", d)
                        ps.after_last("w_stored", d)
                        ps.after_last("v_stored", d)
                        for h in range(HEADS):
                            nc.tensor.transpose(pa[d][:, h * P:(h + 1) * P], kTs[d][:, h, :], k.c("ident"))
                        for h in range(HEADS):
                            last = nc.tensor.transpose(pb[d][:, h * P:(h + 1) * P], vTs[d][:, h, :], k.c("ident"))
                        last.then_inc(s("kv_turned"), 1)
                        ps.after_last("s_done", d)
                        ps.after_last("dt", 2 * (NL - 1) + d)
                        if out:
                            ps.step(NPRE).after_last("o_added", d)
                        nc.tensor.matmul(pd[d][:, 0:4], k.c(f"cum{d}"), gb[d][:, 0:4], start=True, stop=True)
                        for h in range(HEADS):
                            last = nc.tensor.matmul(pc[d][:, h * P:(h + 1) * P], gb[d][:, h:h + 1].to_broadcast([P, P]),
                                                    k.c(f"cum{d}"), start=(h == 0), stop=False, skip_group_check=True)
                        last.then_inc(s("cum"), 1)
                    for d in range(2):
                        ps.after("exp_rows", d)
                        ps.after("cum_read", d)
                        nc.tensor.matmul(pc[d][:, :], k.c("ident"), k.c(f"neg{d}").unsqueeze(1)
                                         .to_broadcast([P, HEADS, P]), start=False, stop=True, skip_group_check=True) \
                            .then_inc(s("neg"), 1)
                        four(pd[d], lambda h: gb[d][:, 4 + h:5 + h].to_broadcast([P, P]), lambda h: k.c("ident")) \
                            .then_inc(s("beta_rows"), 1)
                    for d in range(2):
                        ps.after("kv_scaled", d)
                        four(pa[d], lambda h: kTs[d][:, h, :], lambda h: kTs[d][:, h, :])
                        four(pb[d], lambda h: kTs[d][:, h, :],
                             lambda h: k.cT[:, h, ds(at[d], P)]).then_inc(s("kk"), 1)
                    for d in range(2):
                        ps.after("dt", d)
                        ps.after("lt", d)
                        for h in range(HEADS):
                            last = nc.tensor.transpose(pa[d][:, h * P:(h + 1) * P], dt[d][:, h, :], k.c("ident"))
                        last.then_inc(s("x"), 1)
                    for n in range(1, NL):
                        for d in range(2):
                            ps.after("masked", 2 * n + d)
                            ps.after("d", 2 * (n - 2) + d) if n > 1 else ps.after("d2", d)
                            if n > 1:
                                ps.after("x_stored", 2 * (n - 2) + d)
                            four(pa[d], lambda h: lm[d][:, h, :], lambda h: dm[d][:, h, :]).then_inc(s("x"), 1)
                        for d in range(2):
                            ps.after("x_stored", 2 * (n - 1) + d)
                            ps.after("dt", 2 * (n - 1) + d)
                            if n == 1:
                                ps.after("at", d)
                            if n < NL - 1:
                                four(pb[d], lambda h: dt[d][:, h, :], lambda h: xs[d][:, h, :]).then_inc(s("dx"), 1)
                            four(pc[d], lambda h: xs[d][:, h, :], lambda h: dt[d][:, h, :]).then_inc(s("dxt"), 1)
                    for d in range(2):
                        ps.after("dt", 2 * (NL - 1) + d)
                        four(pa[d], lambda h: kbg[d][:, h, :], lambda h: dt[d][:, h, :]).then_inc(s("w"), 1)
                    for d in range(2):
                        ps.after("w_stored", d)
                        ps.after_last("s_done", d)
                        for h in range(HEADS):
                            nc.tensor.matmul(pb[d][:, h * P:(h + 1) * P], dt[d][:, h, :], vb[d][:, h, :], start=True,
                                             stop=False)
                            last = nc.tensor.matmul(pb[d][:, h * P:(h + 1) * P], wT[d][:, h, :], S[d][:, h, :],
                                                    start=False, stop=True)
                        last.then_inc(s("v"), 1)
                    for d in range(2):
                        ps.after("v_stored", d)
                        if out:
                            ps.after("q_decayed", d)
                            for h in range(HEADS):
                                nc.tensor.matmul(pc[d][:, h * P:(h + 1) * P], S[d][:, h, :], eg[d][:, h, :],
                                                 start=True, stop=False)
                                last = nc.tensor.matmul(pc[d][:, h * P:(h + 1) * P], vn[d][:, h, :], at_[d][:, h, :],
                                                        start=False, stop=True)
                            last.then_inc(s("o"), 1)
                        four(pd[d], lambda h: kd[d][:, h, :], lambda h: vn[d][:, h, :]).then_inc(s("ds"), 1)

                passes(pe, body)

            @block.scalar
            def _(act):
                credit(s, act, per, "exp_rows", "exp_cols", "decayed", "d2", "x_stored", "w_stored")

                def body(it, tile, at, out):
                    ps = Pass(s, act, it, per)
                    for d in range(2):
                        ps.after("cum", d)
                        ps.after_last("ds", d)
                        ps.after_last("q_decayed", d)
                        nc.scalar.activation(eg[d][:, :, :], heads(pc[d][:, :]), ACT.Exp).then_inc(s("exp_rows"), 1)
                    for d in range(2):
                        ps.after("cum_read", d)
                        nc.scalar.activation(sc[d][:, EXC:EXC + 4], sc[d][:, GC:GC + 4], ACT.Exp)
                        nc.scalar.activation(sc[d][:, KDS:KDS + 4], sc[d][:, TOEND:TOEND + 4], ACT.Exp) \
                            .then_inc(s("exp_cols"), 1)
                        ps.after("neg", d)
                        for h in range(HEADS):
                            last = nc.scalar.activation(at_[d][:, h, :], pc[d][:, h * P:(h + 1) * P], ACT.Exp,
                                                        bias=sc[d][:, NGC + h:NGC + h + 1])
                        last.then_inc(s("decayed"), 1)
                    for n in range(NL - 1):
                        for d in range(2):
                            if n == 0:
                                ps.after("x", d)
                                ps.after_last("s_done", d)
                                nc.scalar.activation(dm[d][:, :, :], heads(pa[d][:, :]), ACT.Copy).then_inc(s("d2"), 1)
                        for d in range(2):
                            ps.after("x", 2 * (n + 1) + d)
                            ps.after("dxt", 2 * (n - 1) + d) if n else ps.after("kv_turned", d)
                            nc.scalar.activation(xs[d][:, :, :], heads(pa[d][:, :]), ACT.Copy) \
                                .then_inc(s("x_stored"), 1)
                    for d in range(2):
                        ps.after("w", d)
                        ps.after("x", 2 * (NL - 1) + d)
                        nc.scalar.activation(wT[d][:, :, :], heads(pa[d][:, :]), ACT.Copy, scale=-1.0) \
                            .then_inc(s("w_stored"), 1)

                passes(act, body)

            @block.vector
            def _(dve):
                ch = Chain(dve, s("dve_steps"))
                credit(s, dve, per, "cum_read", "kv_scaled", "lt", "at", "dt", "d", "v_stored", "o_added", "s_done")
                for d in range(2):
                    nc.vector.memset(S[d][:, :, :], 0.0).then_inc(s("zeroed"), 1)
                ch.run(nc.vector.memset(k.oT[:, :, :], 0.0))
                steps = 2 * 3

                def body(it, tile, at, out):
                    ch.enter(it - (NPRE if out else 0), steps)
                    ps = Pass(s, dve, it, per)
                    for d in range(2):
                        v = sc[d]
                        end = P - 1 if d == 0 else 0
                        ps.after("exp_rows", d)
                        ps.after_last("decayed", d)
                        ps.after_last("kv_scaled", d)
                        ps.after_last("s_decayed", d)
                        ch.run(nc.vector.tensor_copy(v[:, GC:GC + 4], pd[d][:, 0:4]))
                        nc.vector.tensor_scalar(v[:, NGC:NGC + 4], v[:, GC:GC + 4], -1.0, None, ALU.mult)
                        nc.vector.tensor_copy(v[:, EGL:EGL + 4], eg[d][:, :, end])
                        nc.vector.tensor_tensor(v[:, TOEND:TOEND + 4], heads(pc[d][:, :])[:, :, end],
                                                v[:, GC:GC + 4], ALU.subtract).then_inc(s("cum_read"), 1)
                    for d in range(2):
                        v = sc[d]
                        ps.after("exp_cols", d)
                        ps.after("kv_turned", d)
                        ch.run(nc.vector.tensor_tensor(v[:, BEG:BEG + 4], v[:, EXC:EXC + 4], gb[d][:, 4:8], ALU.mult))
                        ps.after_last("ds", d)
                        nc.vector.tensor_tensor(kbg[d][:, :, :], heads(pa[d][:, :]), wide(v[:, BEG:BEG + 4]), ALU.mult)
                        nc.vector.tensor_tensor(kd[d][:, :, :], heads(pa[d][:, :]), wide(v[:, KDS:KDS + 4]), ALU.mult)
                        nc.vector.tensor_tensor(vb[d][:, :, :], heads(pb[d][:, :]), wide(gb[d][:, 4:8]), ALU.mult) \
                            .then_inc(s("kv_scaled"), 1)
                    for d in range(2):
                        ps.after("decayed", d)
                        ps.after("beta_rows", d)
                        ps.after("kk", d)
                        ch.run(nc.vector.tensor_tensor(lt[d][:, :, :], heads(pd[d][:, :]), at_[d][:, :, :], ALU.mult))
                        nc.vector.tensor_tensor(lt[d][:, :, :], heads(pa[d][:, :]), lt[d][:, :, :], ALU.mult) \
                            .then_inc(s("lt"), 1)
                        nc.vector.tensor_tensor(at_[d][:, :, :], heads(pb[d][:, :]), at_[d][:, :, :], ALU.mult) \
                            .then_inc(s("at"), 1)
                    for d in range(2):
                        ps.after("masked", d)
                        nc.vector.tensor_tensor(dt[d][:, :, :], k.c("ident").unsqueeze(1).to_broadcast([P, HEADS, P]),
                                                lm[d][:, :, :], ALU.subtract).then_inc(s("dt"), 1)
                    for n in range(1, NL):
                        for d in range(2):
                            if n < NL - 1:
                                ps.after("dx", 2 * (n - 1) + d)
                                nc.vector.tensor_tensor(dm[d][:, :, :], dm[d][:, :, :], heads(pb[d][:, :]),
                                                        ALU.subtract).then_inc(s("d"), 1)
                            ps.after("dxt", 2 * (n - 1) + d)
                            ps.after("dt", 2 * (n - 1) + d)
                            nc.vector.tensor_tensor(dt[d][:, :, :], dt[d][:, :, :], heads(pc[d][:, :]),
                                                    ALU.subtract).then_inc(s("dt"), 1)
                    for d in range(2):
                        ps.after("v", d)
                        ps.after("masked", 2 * (NL - 1) + d)
                        nc.vector.tensor_copy(vn[d][:, :, :], heads(pb[d][:, :])).then_inc(s("v_stored"), 1)
                    for d in range(2):
                        if out:
                            ps.step(NPRE).after("o", d)
                            o = k.oT[:, :, ds(at[d] - LAT, P)]
                            ps.step(NPRE).after("o_added", 0) if d else ps.step(NPRE).after_last("o_added")
                            nc.vector.tensor_tensor(o, o, heads(pc[d][:, :]), ALU.add).then_inc(s("o_added"), 1)
                        ps.after("ds", d)
                        ps.after("s_decayed", d)
                        nc.vector.tensor_tensor(S[d][:, :, :], sd[d][:, :, :], heads(pd[d][:, :]), ALU.add) \
                            .then_inc(s("s_done"), 1)
                    ch.leave(NCH - NPRE if out else NPRE)

                passes(dve, body)


def branches(k):
    nc, dr = k.nc, k.dram
    K31, PAD = 31, 15
    STEPS = 8
    per_in = {"load_a": 1, "load_g": 1, "projected": 4, "glu_sigmoid": 2, "gated": 2}
    per = {"load_g0": 1, "load_g1": 1, "load_b0": 1, "load_b1": 1, "gates": 4, "branches": 4, "sigmoid": 4,
           "product": 4, "convolved": 1}
    with ExitStack() as st:
        s, w = k.brn_signals, k.w_b
        glu = k.sb(st, "glu_sigmoid", [P, 2, 512])
        y = k.sb(st, "gated", [P, KB, SEQ + 2 * PAD])
        taps = k.sb(st, "taps", [P, 32])
        mu = k.sb(st, "mean", [P, SEQ])
        root = mu
        sq = y[:, :, 0:SEQ]
        wg = [k.sb(st, f"w_gate{i}", [P, KD, P]) for i in range(2)]
        wb = [k.sb(st, f"w_branch{i}", [P, KB, P]) for i in range(2)]
        sg = [k.sb(st, f"gate{i}", [P, 512]) for i in range(2)]
        pr = k.sb(st, "product", [P, 2, 512])
        p_w = [k.ps(st, f"p_w{i}", [P, 512]) for i in range(4)]
        p_m, p_v = p_w[0:2], p_w[2:4]
        p_g = [k.ps(st, f"p_gate{i}", [P, 512]) for i in range(2)]
        p_b = [k.ps(st, f"p_branch{i}", [P, 512]) for i in range(2)]
        last_merge = KD

        def items(it, conv_branch):
            if conv_branch:
                return [(1, it * (2 * P)), (1, it * (2 * P) + P)]
            return [(0, it * P), (2, it * P)]

        with nc.Block() as block:
            @block.sync
            def _(sp):
                credit(s, sp, per_in, "load_a", "load_g")
                credit(s, sp, per, "load_g0", "load_g1", "load_b0", "load_b1")
                with sp.Fori(1, KB) as it:
                    ps = Pass(s, sp, it, per_in)
                    src = [w_in_tile(dr, it * P + B_A), w_in_tile(dr, it * P + B_A + BW)]
                    ps.after_last("projected", 3)
                    sp.dma_start(w[0][:], src[0]).then_inc(s("load_a"), 16)
                    sp.dma_start(w[1][:], src[1]).then_inc(s("load_g"), 16)

                def load(ps, it, conv_branch):
                    src = [(w_in_tile(dr, f + (GATES + D * b)),
                            dr["w_branch"][0, b, :, ds(f, P)].rearrange("(c p) n -> p c n", p=P))
                           for b, f in items(it, conv_branch)]
                    for i in range(2):
                        ps.after_last("branches", 2 * i + 1)
                        sp.dma_start(wg[i][:], src[i][0]).then_inc(s(f"load_g{i}"), 16)
                        sp.dma_start(wb[i][:], src[i][1]).then_inc(s(f"load_b{i}"), 16)

                with sp.Fori(0, KD) as it:
                    load(Pass(s, sp, it, per), it, False)
                with sp.Fori(0, KD // 2) as it:
                    load(Pass(s, sp, it, per).step(-last_merge), it, True)

            @block.gpsimd
            def _(pool):
                pool.wait_ge(s("branches"), 4 * (last_merge + 1))
                for half, wo in enumerate(k.w_out):
                    pool.dma_start(wo, dr["w_out"][0, :, 512 * half:512 * half + 512]
                                   .rearrange("(c p) n -> p c n", p=P)).then_inc(k.pout_signals("w_out_loaded", half), 16)

            @block.tensor
            def _(pe):
                credit(s, pe, per_in, "projected")
                credit(s, pe, per, "gates", "branches")
                with pe.Fori(0, KB) as it:
                    ps = Pass(s, pe, it, per_in)
                    for i in range(4):
                        which, half = i % 2, i // 2
                        if i < 2:
                            ps.after(("load_a", "load_g")[which])
                        ps.after_last("gated", half)
                        at = CTX + 512 * half
                        for c in range(KD):
                            last = nc.tensor.matmul(p_w[i][:, :], w[which][:, c, :], k.hT[:, c, at:at + 512],
                                                    start=(c == 0), stop=(c == KD - 1))
                        last.then_inc(s("projected"), 1)

                def merge_pass(ps, ys):
                    for n in range(4):
                        i, half = n // 2, n % 2
                        at = 512 * half
                        if half == 0:
                            ps.after(f"load_g{i}")
                            ps.after(f"load_b{i}")
                        ps.after("product", n - 2) if n >= 2 else ps.after_last("product", 2 + n)
                        for c in range(KD):
                            last = nc.tensor.matmul(p_g[half][:, :], wg[i][:, c, :],
                                                    k.hT[:, c, CTX + at:CTX + at + 512], start=(c == 0),
                                                    stop=(c == KD - 1))
                        last.then_inc(s("gates"), 1)
                        for c in range(KB):
                            last = nc.tensor.matmul(p_b[half][:, :], wb[i][:, c, :], ys[i][:, c, at:at + 512],
                                                    start=(c == 0), stop=(c == KB - 1))
                        last.then_inc(s("branches"), 1)

                def channel_sums(banks, src, name):
                    for half in range(2):
                        for c in range(KB):
                            last = nc.tensor.matmul(banks[half][:, :], k.c("ones"), src[:, c, 512 * half:512 * half + 512],
                                                    start=(c == 0), stop=(c == KB - 1))
                    last.then_inc(s(name), 1)

                others = [k.yaT, k.ycT]
                with pe.Fori(0, KB) as it:
                    merge_pass(Pass(s, pe, it, per), others)
                merge_pass(Pass(s, pe, KB, per), others)
                pe.wait_ge(s("convolved"), KB + 1)
                channel_sums(p_m, k.ybT, "channel_sum")
                merge_pass(Pass(s, pe, KB + 1, per), others)
                pe.wait_ge(s("squared"), 1)
                channel_sums(p_v, sq, "square_sum")
                with pe.Fori(KB + 2, KD) as it:
                    merge_pass(Pass(s, pe, it, per), others)
                pe.wait_ge(s("silu"), 1)
                with pe.Fori(0, KD // 2) as it:
                    merge_pass(Pass(s, pe, it, per).step(-last_merge), [k.ybT, k.ybT])

            @block.scalar
            def _(act):
                credit(s, act, per_in, "glu_sigmoid")
                credit(s, act, per, "sigmoid")
                with act.Fori(0, KB) as it:
                    ps = Pass(s, act, it, per_in)
                    for half in range(2):
                        ps.after("projected", 2 * half + 1)
                        ps.after_last("gated", half)
                        nc.scalar.activation(glu[:, half, :], p_w[2 * half + 1][:, :], ACT.Sigmoid) \
                            .then_inc(s("glu_sigmoid"), 1)

                def merge_pass(ps):
                    for n in range(4):
                        ps.after("gates", n)
                        ps.after("product", n - 2) if n >= 2 else ps.after_last("product", 2 + n)
                        nc.scalar.activation(sg[n % 2][:, :], p_g[n % 2][:, :], ACT.Sigmoid).then_inc(s("sigmoid"), 1)

                with act.Fori(0, KB + 1) as it:
                    merge_pass(Pass(s, act, it, per))
                act.wait_ge(s("channel_sum"), 1)
                for half in range(2):
                    nc.scalar.activation(mu[:, 512 * half:512 * half + 512], p_m[half][:, :], ACT.Copy,
                                         scale=1.0 / BW).then_inc(s("mean"), 1)
                act.wait_ge(s("centred"), 1)
                nc.scalar.activation(sq, k.ybT[:, :, :], ACT.Square).then_inc(s("squared"), 1)
                merge_pass(Pass(s, act, KB + 1, per))
                act.wait_ge(s("square_sum"), 1)
                for half in range(2):
                    nc.scalar.activation(root[:, 512 * half:512 * half + 512], p_v[half][:, :], ACT.Sqrt,
                                         bias=k.eps[:, 1:2], scale=1.0 / BW).then_inc(s("rooted"), 1)
                merge_pass(Pass(s, act, KB + 2, per))
                act.wait_ge(s("scaled"), 1)
                for c in range(KB):
                    nc.scalar.activation(sq[:, c, :], k.ybT[:, c, :], ACT.Identity, bias=k.col("conv_ln_b", c),
                                         scale=k.col("conv_ln_w", c)).then_inc(s("affine"), 1)
                act.wait_ge(s("affine"), KB)
                nc.scalar.activation(k.ybT[:, :, :], sq, ACT.Sigmoid).then_inc(s("affine_sigmoid"), 1)
                merge_pass(Pass(s, act, KB + 3, per))
                with act.Fori(0, KD // 2) as it:
                    merge_pass(Pass(s, act, it, per).step(-last_merge))

            @block.vector
            def _(dve):
                ch = Chain(dve, s("dve_steps"))
                credit(s, dve, per_in, "gated")
                credit(s, dve, per, "product", "convolved")
                ch.run(nc.vector.memset(y[:, :, 0:PAD], 0.0))
                ch.run(nc.vector.memset(y[:, :, PAD + SEQ:], 0.0))
                with dve.Fori(0, KB) as it:
                    ps = Pass(s, dve, it, per_in)
                    for half in range(2):
                        ps.after("glu_sigmoid", half)
                        dst = y[:, ds(it, 1), PAD + 512 * half:PAD + 512 * half + 512].rearrange("p a n -> p (a n)")
                        nc.vector.tensor_tensor(dst, p_w[2 * half][:, :], glu[:, half, :], ALU.mult) \
                            .then_inc(s("gated"), 1)
                dve.wait_ge(s("gated"), 2 * (KB + 1))

                def add_product(ps, n, it, conv_branch):
                    half = n % 2
                    tile = it * 2 + n // 2 if conv_branch else it
                    m = k.mT[:, ds(tile, 1), 512 * half:512 * half + 512].rearrange("p a n -> p (a n)")
                    ps.after("branches", n)
                    ps.after("sigmoid", n)
                    first = not conv_branch and n < 2
                    nc.vector.tensor_tensor(m if first else pr[:, half, :], p_b[half][:, :], sg[half][:, :], ALU.mult) \
                        .then_inc(s("product"), 1)
                    if not first:
                        ps.after("product", n)
                        ch.run(nc.vector.tensor_tensor(m, m, pr[:, half, :], ALU.add))

                with dve.Fori(0, KB) as it:
                    ch.enter(it, 2 + K31 - 1 + 2)
                    ps = Pass(s, dve, it, per)
                    ps.after_last("convolved")
                    ch.run(nc.vector.tensor_copy(taps[:, 0:K31], k.taps31[:, :].rearrange("p (t c) -> p t c", c=KB)
                                                 [:, :, ds(it, 1)].rearrange("p t a -> p (t a)")))
                    nb = VEC["conv_dw_b"][0]
                    ch.run(nc.vector.tensor_copy(taps[:, K31:K31 + 1], k.vec[:, ds(it + nb, 1)]))
                    o = k.ybT[:, ds(it, 1), :].rearrange("p a n -> p (a n)")

                    def shifted(t):
                        return y[:, ds(it, 1), t:t + SEQ].rearrange("p a n -> p (a n)")

                    for n in range(4):
                        for t in range(STEPS * n, min(STEPS * (n + 1), K31)):
                            if t == 0:
                                ch.run(nc.vector.tensor_scalar(o, shifted(0), taps[:, 0:1], taps[:, K31:K31 + 1],
                                                               ALU.mult, ALU.add))
                                continue
                            ins = nc.vector.scalar_tensor_tensor(o, shifted(t), taps[:, t:t + 1], o, ALU.mult, ALU.add)
                            if t < K31 - 1:
                                ch.run(ins)
                            else:
                                ins.then_inc(s("convolved"), 1)
                        add_product(ps, n, it, False)
                ch.leave(KB)

                def merge_pass(ps, it, conv_branch):
                    for n in range(4):
                        add_product(ps, n, it, conv_branch)

                def over_channels(row):
                    return row[:, :].unsqueeze(1).to_broadcast([P, KB, SEQ])

                yb = k.ybT[:, :, :]
                merge_pass(Pass(s, dve, KB, per), KB, False)
                dve.wait_ge(s("mean"), 2)
                nc.vector.tensor_tensor(yb, yb, over_channels(mu), ALU.subtract).then_inc(s("centred"), 1)
                merge_pass(Pass(s, dve, KB + 1, per), KB + 1, False)
                dve.wait_ge(s("rooted"), 2)
                ch.run(nc.vector.reciprocal(root[:, :], root[:, :]))
                nc.vector.tensor_tensor(yb, yb, over_channels(root), ALU.mult).then_inc(s("scaled"), 1)
                merge_pass(Pass(s, dve, KB + 2, per), KB + 2, False)
                dve.wait_ge(s("affine_sigmoid"), 1)
                nc.vector.tensor_tensor(yb, yb, sq, ALU.mult).then_inc(s("silu"), 1)
                merge_pass(Pass(s, dve, KB + 3, per), KB + 3, False)
                with dve.Fori(0, KD // 2) as it:
                    ch.enter(it, 4)
                    merge_pass(Pass(s, dve, it, per).step(-last_merge), it, True)
                ch.leave(KD // 2)


def project_out(k):
    nc, dr = k.nc, k.dram
    per = {"load_x": 1, "staged": 1, "projected": 1, "gated": 1, "x1": 1, "load_x1_out": 1, "squared": 1, "rooted": 1,
           "xn": 1, "load_xn_out": 1, "turned": 1, "modulated": 1, "routed": 1, "logits": 1}
    with ExitStack() as st:
        s, wo = k.pout_signals, k.w_out
        rw = k.sb(st, "router_w", [P, KD, N_EXP])
        mt = k.sb(st, "m_tile", [P, KD, P])
        x = k.sb(st, "x", [P, D])
        x1 = k.sb(st, "x1", [P, D])
        xn = k.sb(st, "xn", [P, D])
        h2 = k.sb(st, "h2T", [P, KD, P])
        sq = k.sb(st, "sq", [P, D])
        ssum = k.sb(st, "square_sum", [P, 1])
        root = k.sb(st, "root", [P, 1])
        rinv = k.sb(st, "inverse", [P, 1])
        p_o = k.ps(st, "p_out", [P, D])
        p_t = k.ps(st, "p_turned", [P, D])
        p_r = k.ps(st, "p_router", [P, 512])

        with nc.Block() as block:
            @block.sync
            def _(sp):
                credit(s, sp, per, "load_x", "load_x1_out", "load_xn_out")
                sp.dma_start(rw[:], dr["router_w"].rearrange("(c p) n -> p c n", p=P)).then_inc(s("router_loaded"), 16)
                with sp.Fori(0, SEQ // P) as it:
                    ps = Pass(s, sp, it, per)
                    src = dr["x"][0, ds(it * P, P), :]
                    d1, dn = dr["x1"][ds(it * P, P), :], dr["xn"][ds(it * P, P), :]
                    ps.after_last("x1")
                    sp.dma_start(x[:], src).then_inc(s("load_x"), 16)
                    ps.after("x1")
                    sp.dma_start(d1, x1[:]).then_inc(s("load_x1_out"), 16)
                    ps.after("xn")
                    sp.dma_start(dn, xn[:]).then_inc(s("load_xn_out"), 16)
                sp.wait_ge(s("load_x1_out"), 16 * (SEQ // P + 1))
                sp.wait_ge(s("load_xn_out"), 16 * (SEQ // P + 1))

            @block.gpsimd
            def _(pool):
                credit(s, pool, per, "staged")
                with pool.Fori(0, SEQ // P) as it:
                    ps = Pass(s, pool, it, per)
                    ps.after_last("projected")
                    nc.gpsimd.tensor_copy(mt[:, :, :], k.mT[:, :, ds(it * P, P)]).then_inc(s("staged"), 1)

            @block.tensor
            def _(pe):
                credit(s, pe, per, "projected", "turned", "routed")
                for half in range(2):
                    pe.wait_ge(s("w_out_loaded", half), 16)
                pe.wait_ge(s("router_loaded"), 16)
                first = Pass(s, pe, 0, per)

                def project(ps, half):
                    if half == 0:
                        ps.after("staged")
                        ps.after_last("gated")
                    for c in range(KD):
                        last = nc.tensor.matmul(p_o[:, 512 * half:512 * half + 512], mt[:, c, :],
                                                wo[half][:, c, :], start=(c == 0),
                                                stop=(c == KD - 1))
                    if half:
                        last.then_inc(s("projected"), 1)

                def turn(ps):
                    ps.after("xn")
                    ps.after_last("modulated")
                    for c in range(KD):
                        last = nc.tensor.transpose(p_t[:, c * P:(c + 1) * P], xn[:, c * P:(c + 1) * P], k.c("ident"))
                    last.then_inc(s("turned"), 1)

                def route_rows(ps):
                    ps.after("modulated")
                    ps.after_last("logits")
                    for c in range(KD):
                        last = nc.tensor.matmul(p_r[:, 0:N_EXP], h2[:, c, :], rw[:, c, :], start=(c == 0),
                                                stop=(c == KD - 1))
                    last.then_inc(s("routed"), 1)

                project(first, 0)
                project(first, 1)
                with pe.Fori(0, SEQ // P - 1) as it:
                    ps = Pass(s, pe, it, per)
                    ahead = ps.step(-1)
                    project(ahead, 0)
                    turn(ps)
                    project(ahead, 1)
                    route_rows(ps)
                end = Pass(s, pe, SEQ // P - 1, per)
                turn(end)
                route_rows(end)

            @block.scalar
            def _(act):
                credit(s, act, per, "squared", "rooted", "logits")
                with act.Fori(0, SEQ // P) as it:
                    ps = Pass(s, act, it, per)
                    ps.after("x1")
                    ps.after_last("rooted")
                    nc.scalar.activation(sq[:, :], x1[:, :], ACT.Square, accum_out=ssum[:, :]).then_inc(s("squared"), 1)
                    ps.after("squared")
                    ps.after_last("xn")
                    nc.scalar.activation(root[:, :], ssum[:, :], ACT.Sqrt, bias=k.eps[:, 0:1], scale=1.0 / D) \
                        .then_inc(s("rooted"), 1)
                    ps.after("routed")
                    nc.scalar.activation(k.scores[:, ds(it, 1), :].rearrange("p a n -> p (a n)"), p_r[:, 0:N_EXP],
                                         ACT.Sigmoid).then_inc(s("logits"), 1)

            @block.vector
            def _(dve):
                ch = Chain(dve, s("dve_steps"))
                credit(s, dve, per, "gated", "x1", "xn", "modulated")
                with dve.Fori(0, SEQ // P) as it:
                    ch.enter(it, 2)
                    ps = Pass(s, dve, it, per)
                    ps.after("projected")
                    ps.after_last("squared")
                    ps.after_last("load_x1_out")
                    nc.vector.tensor_tensor(x1[:, :], p_o[:, :], k.g1b[:, :], ALU.mult).then_inc(s("gated"), 1)
                    ps.after("gated")
                    ps.after("load_x")
                    nc.vector.tensor_tensor(x1[:, :], x1[:, :], x[:, :], ALU.add).then_inc(s("x1"), 1)
                    ps.after("rooted")
                    ch.run(nc.vector.reciprocal(rinv[:, :], root[:, :]))
                    ps.after_last("load_xn_out")
                    ps.after_last("turned")
                    nc.vector.tensor_scalar(xn[:, :], x1[:, :], rinv[:, 0:1], None, ALU.mult).then_inc(s("xn"), 1)
                    ps.after("turned")
                    ps.after_last("routed")
                    ch.run(nc.vector.tensor_tensor(h2[:, :, :], p_t[:, :].rearrange("p (c n) -> p c n", c=KD),
                                                   k.a2[:, :, 0:1].to_broadcast([P, KD, P]), ALU.mult))
                    nc.vector.tensor_tensor(h2[:, :, :], h2[:, :, :], k.mod[:, 3 * KD:4 * KD, 0:1]
                                            .to_broadcast([P, KD, P]), ALU.add).then_inc(s("modulated"), 1)
                ch.leave(SEQ // P)


def route(k):
    nc, dr = k.nc, k.dram
    NT, G, E = SEQ // P, 4, 4
    BIG = float(1 << 20)
    with ExitStack() as st:
        s = Signals(nc, st, "rt")
        biased = k.sb(st, "biased", [P, NT, N_EXP])
        rank = k.sb(st, "rank", [P, NT * G, E])
        ge = k.sb(st, "not_less", [P, NT * G])
        top = k.sb(st, "top_two", [P, NT * G, E])
        gsum = k.sb(st, "group_sum", [P, NT, G])
        grank = k.sb(st, "group_rank", [P, NT, G])
        sel = k.sb(st, "chosen", [P, NT, N_EXP])
        w = k.sb(st, "weights", [P, NT, N_EXP])
        wsum = k.sb(st, "weight_sum", [P, NT])
        tot = k.sb(st, "tile_totals", [P, NT, N_EXP])
        before = k.sb(st, "before_tile", [P, NT + 1, N_EXP])
        nblk = k.sb(st, "blocks", [P, N_EXP])
        upto = k.sb(st, "blocks_up_to", [P, N_EXP])
        dest = k.sb(st, "place", [P, NT, N_EXP])
        tmp = k.sb(st, "tmp", [P, NT, N_EXP])
        d = [k.sb(st, f"row{i}", [P, NT]) for i in range(2)]
        ones16 = k.sb(st, "ones16", [P, N_EXP])
        starts = k.sb(st, "starts", [P, N_EXP + 2])
        zero = k.sb(st, "zero_tokens", [P, N_BLK], I32)
        tok = k.sb(st, "token_numbers", [P, NT], I32)
        by_block = k.sb(st, "tokens_by_block", [N_BLK, P], I32)
        by_block_f = k.sb(st, "tokens_by_block_float", [N_BLK, P])
        p_in = k.ps(st, "p_within", [P, 512])
        p_tot = k.ps(st, "p_totals", [P, 512])

        with nc.Block() as block:
            @block.gpsimd
            def _(pool):
                nc.gpsimd.memset(zero[:, :], 0).then_inc(s("zeroed"), 1)
                nc.gpsimd.memset(k.block_tok[:, N_BLK:N_BLK + 1], 0).then_inc(s("zeroed"), 1)
                nc.gpsimd.iota(tok[:, :], pattern=[[P, NT]], base=0, channel_multiplier=1).then_inc(s("numbered"), 1)
                pool.wait_ge(s("numbered"), 1)
                pool.wait_ge(s("cleared"), 16)
                pool.wait_ge(s("rows_found"), 2)
                for t in range(NT):
                    for i in range(2):
                        nc.gpsimd.indirect_dma_start(
                            dr["tokens"][:, :], bass.IndirectOffsetOnAxis(ap=k.row[i][:, t:t + 1], axis=0),
                            tok[:, t:t + 1], None).then_inc(s("scattered"), 16)

            @block.sync
            def _(sp):
                sp.wait_ge(s("zeroed"), 2)
                sp.dma_start(dr["tokens"].rearrange("(p b) a -> p (b a)", p=P), zero[:, :]).then_inc(s("cleared"), 16)
                sp.dma_start(k.w_gate[0][:], dr["w_gate"][0, 0].rearrange("(c p) n -> p c n", p=P)) \
                    .then_inc(k.exp_signals("gate_loaded", 0), 16)
                sp.wait_ge(s("cleared"), 16)
                sp.wait_ge(s("scattered"), 16 * 2 * NT)
                sp.dma_start(by_block[:, :], dr["tokens"].rearrange("(b p) a -> b (p a)", p=P)) \
                    .then_inc(s("blocks_loaded"), 16)

            @block.tensor
            def _(pe):
                pe.wait_ge(s("chosen"), 1)
                flat = sel[:, :, :].rearrange("p t e -> p (t e)")
                nc.tensor.matmul(p_in[:, 0:P], k.c("tri"), flat, start=True, stop=True)
                nc.tensor.matmul(p_tot[:, 0:P], k.c("ones"), flat, start=True, stop=True).then_inc(s("counted"), 1)
                pe.wait_ge(s("blocks_float"), 1)
                nc.tensor.transpose(p_tot[:, 0:N_BLK], by_block_f[:, :], k.c("ident")[0:N_BLK, 0:N_BLK]) \
                    .then_inc(s("blocks_turned"), 1)

            @block.vector
            def _(dve):
                ch = Chain(dve, s("dve_steps"))
                V = nc.vector
                four = biased[:, :, :].rearrange("p t (g e) -> p (t g) e", e=E)
                bias = k.rows[:, 16:32].unsqueeze(1).to_broadcast([P, NT, N_EXP])
                ch.run(V.tensor_tensor(biased[:, :, :], k.scores[:, :, :], bias, ALU.add))

                def ranks(r, v, c, n):
                    for i in range(n):
                        ch.run(V.memset(r(i), float(n - 1 - i)))
                    for i in range(n):
                        for jj in range(i):
                            ch.run(V.tensor_tensor(c, v(jj), v(i), ALU.is_ge))
                            ch.run(V.tensor_tensor(r(i), r(i), c, ALU.add))
                            ch.run(V.tensor_tensor(r(jj), r(jj), c, ALU.subtract))

                ranks(lambda i: rank[:, :, i], lambda i: four[:, :, i], ge[:, :], E)
                ch.run(V.tensor_scalar(rank[:, :, :], rank[:, :, :], 2.0, None, ALU.is_lt))
                ch.run(V.tensor_tensor(top[:, :, :], rank[:, :, :], four, ALU.mult))
                ch.run(V.tensor_reduce(gsum[:, :, :].rearrange("p t g -> p (t g)"), top[:, :, :], AX.X, ALU.add))
                ranks(lambda i: grank[:, :, i], lambda i: gsum[:, :, i], ge[:, 0:NT], G)
                ch.run(V.tensor_scalar(grank[:, :, :], grank[:, :, :], 1.0, None, ALU.is_lt))
                V.tensor_tensor(sel[:, :, :].rearrange("p t (g e) -> p (t g) e", e=E), rank[:, :, :],
                                grank[:, :, :].rearrange("p t g -> p (t g)").unsqueeze(2)
                                .to_broadcast([P, NT * G, E]), ALU.mult).then_inc(s("chosen"), 1)
                dve.wait_ge(s("chosen"), 1)
                ch.run(V.tensor_tensor(w[:, :, :], k.scores[:, :, :], sel[:, :, :], ALU.mult))
                dve.wait_ge(s("counted"), 1)
                ch.run(V.tensor_copy(tot[:, :, :], p_tot[:, 0:P].rearrange("p (t e) -> p t e", e=N_EXP)))
                ch.run(V.memset(before[:, 0, :], 0.0))
                for t in range(NT):
                    ch.run(V.tensor_tensor(before[:, t + 1, :], before[:, t, :], tot[:, t, :], ALU.add))
                ch.run(V.memset(nblk[:, :], 1.0))
                for m in range(1, NT):
                    ch.run(V.scalar_tensor_tensor(nblk[:, :], before[:, NT, :], float(m * P), nblk[:, :], ALU.is_gt,
                                                  ALU.add))
                ch.run(V.memset(ones16[:, :], 1.0))
                ch.run(V.tensor_tensor_scan(upto[:, :], ones16[:, :], nblk[:, :], 0.0, ALU.mult, ALU.add))
                ch.run(V.memset(starts[:, 0:2], 0.0))
                ch.run(V.tensor_copy(starts[:, 2:], upto[:, :]))
                ch.run(V.tensor_copy(k.starts[:, :], starts[:, :]))
                ch.run(V.tensor_tensor(dest[:, :, :], p_in[:, 0:P].rearrange("p (t e) -> p t e", e=N_EXP),
                                       before[:, 0:NT, :], ALU.add))
                ch.run(V.tensor_scalar(ones16[:, :], starts[:, 1:N_EXP + 1], float(P), None, ALU.mult))
                ch.run(V.tensor_tensor(dest[:, :, :], dest[:, :, :], ones16[:, :].unsqueeze(1)
                                       .to_broadcast([P, NT, N_EXP]), ALU.add))
                ch.run(V.tensor_tensor(tmp[:, :, :], dest[:, :, :], sel[:, :, :], ALU.mult))
                ch.run(V.tensor_reduce(d[1][:, :], tmp[:, :, :], AX.X, ALU.max))
                ch.run(V.tensor_scalar(sel[:, :, :], sel[:, :, :], -BIG, BIG, ALU.mult, ALU.add))
                ch.run(V.tensor_tensor(tmp[:, :, :], tmp[:, :, :], sel[:, :, :], ALU.add))
                ch.run(V.tensor_reduce(d[0][:, :], tmp[:, :, :], AX.X, ALU.min))
                for i in range(2):
                    V.tensor_copy(k.row[i][:, :], d[i][:, :]).then_inc(s("rows_found"), 1)
                ch.run(V.tensor_reduce(wsum[:, :], w[:, :, :], AX.X, ALU.add))
                ch.run(V.reciprocal(wsum[:, :], wsum[:, :]))
                ch.run(V.tensor_tensor(w[:, :, :], w[:, :, :], wsum[:, :].unsqueeze(2).to_broadcast([P, NT, N_EXP]),
                                       ALU.mult))
                for i in range(2):
                    ch.run(V.tensor_tensor(tmp[:, :, :], dest[:, :, :], d[i][:, :].unsqueeze(2)
                                           .to_broadcast([P, NT, N_EXP]), ALU.is_equal))
                    ch.run(V.tensor_tensor(tmp[:, :, :], tmp[:, :, :], w[:, :, :], ALU.mult))
                    ch.run(V.tensor_reduce(k.weight[i][:, :], tmp[:, :, :], AX.X, ALU.add))
                dve.wait_ge(s("blocks_loaded"), 16)
                V.tensor_copy(by_block_f[:, :], by_block[:, :]).then_inc(s("blocks_float"), 1)
                dve.wait_ge(s("blocks_turned"), 1)
                ch.run(V.tensor_copy(k.block_tok[:, 0:N_BLK], p_tot[:, 0:N_BLK]))


def experts(k):
    nc, dr = k.nc, k.dram
    HALF = D // 2
    with ExitStack() as st:
        s = k.exp_signals
        wg = k.w_gate
        wu = k.sb(st, "w_up", [P, KD, D])
        wd = [k.sb(st, f"w_down{i}", [P, KD, D]) for i in range(2)]
        cur = k.sb(st, "tokens", [P, 1], I32)
        xg = k.sb(st, "rows", [P, D])
        xT = k.sb(st, "rowsT", [P, KD, P])
        sg = k.sb(st, "sigmoid", [P, D])
        hT = k.sb(st, "hiddenT", [P, D])
        y = k.sb(st, "y", [P, D])
        p_g = k.ps(st, "p_gate", [P, D])
        p_u = k.ps(st, "p_up", [P, D])
        p_y = k.ps(st, "p_y", [P, D])
        p_t = k.ps(st, "p_turned", [P, D])

        def blocks(eng):
            n = eng.value_load(k.starts[0:1, N_EXP + 1:N_EXP + 2], min_val=N_EXP, max_val=N_BLK - 1)
            return n

        with nc.Block() as block:
            @block.sync
            def _(sp):
                def weights(name, e):
                    return dr[name][0, ds(e, 1), :, :].rearrange("a (c p) n -> p (a c) n", p=P)

                def load(pair, par, last=False):
                    e = pair * 2 + par
                    src = [weights("w_up", e), weights("w_down", e)] + ([] if last else [weights("w_gate", e + 1)])
                    two = sp.value_load(k.starts[0:1, ds(e, 1)], min_val=0, max_val=N_BLK - 1)
                    one = sp.value_load(k.starts[0:1, ds(e + 1, 1)], min_val=0, max_val=N_BLK - 1)
                    done2, done1 = sp.snap(two + 1), sp.snap(one + 1)
                    sp.wait_ge(s("ups"), done1)
                    sp.dma_start(wu[:], src[0]).then_inc(s("up_loaded"), 16)
                    sp.wait_ge(s("downs"), done2)
                    sp.dma_start(wd[par][:], src[1]).then_inc(s("down_loaded", par), 16)
                    if not last:
                        sp.wait_ge(s("gates"), done1)
                        sp.dma_start(wg[1 - par][:], src[2]).then_inc(s("gate_loaded", 1 - par), 16)
                    else:
                        sp.wait_ge(s("gates"), done1)
                        sp.dma_start(wg[1 - par][:], dr["x1"].rearrange("(t p) n -> p t n", p=P)) \
                            .then_inc(s("x1_loaded"), 16)

                sp.wait_ge(s("gathered"), 16)
                with sp.Fori(0, N_EXP // 2 - 1) as pair:
                    load(pair, 0)
                    load(pair, 1)
                load(N_EXP // 2 - 1, 0)
                load(N_EXP // 2 - 1, 1, last=True)

            @block.gpsimd
            def _(pool):
                def fetch(column):
                    nc.gpsimd.tensor_copy(cur[:, :], column).then_inc(s("tokens_ready"), 1)

                def gather():
                    nc.gpsimd.indirect_dma_start(xg[:, :], None, dr["xn"][:, :],
                                                 bass.IndirectOffsetOnAxis(ap=cur[:, 0:1], axis=0)) \
                        .then_inc(s("gathered"), 16)

                n = blocks(pool)
                fetch(k.block_tok[:, 0:1])
                pool.wait_ge(s("tokens_ready"), 1)
                gather()
                with pool.Fori(0, n) as g:
                    pool.wait_ge(s("gathered"), g * 16 + 16)
                    fetch(k.block_tok[:, ds(g + 1, 1)])
                    pool.wait_ge(s("tokens_ready"), g + 2)
                    pool.wait_ge(s("turned"), g + 1)
                    pool.sem_inc(s("gathers_begun"), 1)
                    gather()
                last = pool.snap(n * 16 + 16)
                pool.wait_ge(s("gathered"), last)

            @block.tensor
            def _(pe):
                pe.sem_inc(s("gates"), 1)
                pe.sem_inc(s("ups"), 1)
                pe.sem_inc(s("downs"), 1)

                def turn(g):
                    pe.wait_ge(s("gathered"), g * 16 + 16)
                    for c in range(KD):
                        last = nc.tensor.transpose(p_t[:, c * P:(c + 1) * P], xg[:, c * P:(c + 1) * P], k.c("ident"))
                    last.then_inc(s("turned"), 1)

                turn(0)
                with pe.Fori(0, N_EXP // 2) as pair:
                    for par in range(2):
                        e = pair * 2 + par
                        first = pe.value_load(k.starts[0:1, ds(e + 1, 1)], min_val=0, max_val=N_BLK - 1)
                        end = pe.value_load(k.starts[0:1, ds(e + 2, 1)], min_val=1, max_val=N_BLK - 1)
                        with pe.Fori(first, end) as g:
                            pe.wait_ge(s("modulated"), g * 2 + 2)
                            pe.wait_ge(s("gate_loaded", par), pair * 16 + 16)
                            pe.wait_ge(s("gated"), g + 1)
                            for f in range(KD):
                                for c in range(KD):
                                    last = nc.tensor.matmul(p_g[:, f * P:(f + 1) * P], wg[par][:, c, f * P:(f + 1) * P],
                                                            xT[:, c, :], start=(c == 0), stop=(c == KD - 1))
                            last.then_inc(s("gates"), 1)
                            pe.wait_ge(s("up_loaded"), pair * 32 + (par + 1) * 16)
                            pe.wait_ge(s("hidden"), g * 2 + 2)
                            for f in range(KD):
                                for c in range(KD):
                                    last = nc.tensor.matmul(p_u[:, f * P:(f + 1) * P], wu[:, c, f * P:(f + 1) * P],
                                                            xT[:, c, :], start=(c == 0), stop=(c == KD - 1))
                                if f == KD // 2 - 1:
                                    last.then_inc(s("first_ups"), 1)
                            last.then_inc(s("ups"), 1)
                            turn(g + 1)
                            pe.wait_ge(s("down_loaded", par), pair * 16 + 16)
                            pe.wait_ge(s("hidden"), g * 2 + 4)
                            pe.wait_ge(s("y_stored"), g + 1)
                            for half in range(2):
                                for c in range(KD):
                                    last = nc.tensor.matmul(p_y[:, half * HALF:(half + 1) * HALF],
                                                            hT[:, c * P:(c + 1) * P],
                                                            wd[par][:, c, half * HALF:(half + 1) * HALF],
                                                            start=(c == 0), stop=(c == KD - 1))
                            last.then_inc(s("downs"), 1)

            @block.scalar
            def _(act):
                act.sem_inc(s("y_stored"), 1)
                act.sem_inc(s("y_out"), 16)
                n = blocks(act)

                def modulate(g):
                    act.wait_ge(s("turned"), g + 1)
                    act.wait_ge(s("ups"), g + 1)
                    for c in range(KD // 2):
                        last = nc.scalar.activation(xT[:, c, :], p_t[:, c * P:(c + 1) * P], ACT.Identity,
                                                    bias=k.mod[:, 3 * KD + c, 0:1], scale=k.a2[:, c, 0:1])
                    last.then_inc(s("modulated"), 1)

                modulate(0)
                act.wait_ge(s("y_zeroed"), 1)
                with act.Fori(n, N_BLK) as g:
                    act.dma_start(dr["expert_rows"][ds(g * P, P), :], y[:, :]).then_inc(s("filled"), 16)
                with act.Fori(0, n):
                    act.sem_inc(s("filled"), 16)
                with act.Fori(0, n) as g:
                    rows = dr["expert_rows"][ds(g * P, P), :]
                    act.wait_ge(s("gates"), g + 2)
                    act.wait_ge(s("hidden"), g * 2 + 2)
                    nc.scalar.activation(sg[:, :], p_g[:, :], ACT.Sigmoid).then_inc(s("sigmoid"), 1)
                    modulate(g + 1)
                    act.wait_ge(s("downs"), g + 2)
                    act.wait_ge(s("filled"), 16 * N_BLK)
                    act.wait_ge(s("y_out"), g * 16 + 16)
                    nc.scalar.activation(y[:, :], p_y[:, :], ACT.Copy).then_inc(s("y_stored"), 1)
                    act.wait_ge(s("y_stored"), g + 2)
                    act.dma_start(rows, y[:, :]).then_inc(s("y_out"), 16)
                last = act.snap(n * 16 + 16)
                act.wait_ge(s("y_out"), last)
                act.sem_inc(s("all_out"), 1)

            @block.vector
            def _(dve):
                dve.sem_inc(s("gated"), 1)
                dve.sem_inc(s("hidden"), 2)
                nc.vector.memset(y[:, :], 0.0).then_inc(s("y_zeroed"), 1)
                n = blocks(dve)

                def modulate(g):
                    dve.wait_ge(s("turned"), g + 1)
                    dve.wait_ge(s("ups"), g + 1)
                    for c in range(KD // 2, KD):
                        last = nc.vector.tensor_scalar(xT[:, c, :], p_t[:, c * P:(c + 1) * P], k.a2[:, c, 0:1],
                                                       k.mod[:, 3 * KD + c, 0:1], ALU.mult, ALU.add)
                    last.then_inc(s("modulated"), 1)

                modulate(0)
                with dve.Fori(0, n) as g:
                    dve.wait_ge(s("sigmoid"), g + 1)
                    nc.vector.tensor_tensor(sg[:, :], p_g[:, :], sg[:, :], ALU.mult).then_inc(s("gated"), 1)
                    dve.wait_ge(s("gated"), g + 2)
                    dve.wait_ge(s("downs"), g + 1)
                    for half in range(2):
                        if half:
                            dve.wait_ge(s("ups"), g + 2)
                        else:
                            dve.wait_ge(s("first_ups"), g + 1)
                        part = slice(half * HALF, (half + 1) * HALF)
                        nc.vector.tensor_tensor(hT[:, part], p_u[:, part], sg[:, part], ALU.mult) \
                            .then_inc(s("hidden"), 1)
                    modulate(g + 1)


def combine(k):
    nc, dr = k.nc, k.dram
    NT = SEQ // P
    x1 = k.w_gate[0]
    with ExitStack() as st:
        s = Signals(nc, st, "cmb")
        y = [[k.sb(st, f"y{i}{t}", [P, D]) for i in range(2)] for t in range(NT)]

        with nc.Block() as block:
            @block.gpsimd
            def _(pool):
                for t in range(NT):
                    for i in range(2):
                        nc.gpsimd.indirect_dma_start(
                            y[t][i][:, :], None, dr["expert_rows"][:, :],
                            bass.IndirectOffsetOnAxis(ap=k.row[i][:, t:t + 1], axis=0)) \
                            .then_inc(s(f"rows{i}_loaded", t), 16)

            @block.scalar
            def _(act):
                for t in range(NT):
                    act.wait_ge(s("rows0_loaded", t), 16)
                    nc.scalar.activation(y[t][0][:, :], y[t][0][:, :], ACT.Copy, scale=k.weight[0][:, t:t + 1]) \
                        .then_inc(s("weighted"), 1)

            @block.vector
            def _(dve):
                ch = Chain(dve, s("dve_steps"))
                dve.wait_ge(k.exp_signals("x1_loaded"), 16)
                for t in range(NT):
                    a, b = y[t]
                    dve.wait_ge(s("rows1_loaded", t), 16)
                    dve.wait_ge(s("weighted"), t + 1)
                    ch.run(nc.vector.scalar_tensor_tensor(a[:, :], b[:, :], k.weight[1][:, t:t + 1], a[:, :], ALU.mult,
                                                          ALU.add))
                    ch.run(nc.vector.tensor_tensor(a[:, :], a[:, :], k.g2b[:, :], ALU.mult))
                    nc.vector.tensor_tensor(a[:, :], a[:, :], x1[:, t, :], ALU.add).then_inc(s("done"), 1)

            @block.sync
            def _(sp):
                for t in range(NT):
                    sp.wait_ge(s("done"), t + 1)
                    sp.dma_start(dr["out"][0, t * P:(t + 1) * P, :], y[t][0][:, :]).then_inc(s("out"), 16)
                sp.wait_ge(s("out"), 16 * NT)


INPUTS = ["x", "c", "ctx", "c_ctx", "w_mod", "b_mod", "norm1_w", "norm2_w", "w_in", "qn_w", "kn_w", "lam_p", "subln_w",
          "conv_dw_w", "conv_dw_b", "conv_ln_w", "conv_ln_b", "gdn_conv_w", "gdn_a_log", "gdn_dt_bias", "gdn_norm_w",
          "w_branch", "w_out", "router_w", "router_bias", "w_gate", "w_up", "w_down"]


def allocate(k, st):
    k.const = k.sb(st, "const", [P, CONST_W])
    k.eps = k.sb(st, "eps", [P, 2])
    k.vec = k.sb(st, "vec", [P, VEC_N])
    k.taps31 = k.sb(st, "taps31", [P, 124])
    k.taps5 = k.sb(st, "taps5", [P, 60])
    k.rows = k.sb(st, "rows", [P, 33])
    k.mod = k.sb(st, "mod", [P, 48, 2])
    k.mod_done = k.sb(st, "mod_done", [P, 2])
    k.a1 = k.sb(st, "a1", [P, KD, 2])
    k.a2 = k.sb(st, "a2", [P, KD, 2])
    k.g1b = k.sb(st, "g1b", [P, D])
    k.g2b = k.sb(st, "g2b", [P, D])
    k.scores = k.sb(st, "scores", [P, SEQ // P, N_EXP])
    k.starts = k.sb(st, "starts_int", [P, N_EXP + 2], I32)
    k.block_tok = k.sb(st, "block_tokens", [P, N_BLK + 1], I32)
    k.row = [k.sb(st, f"row_of_choice{i}", [P, SEQ // P], I32) for i in range(2)]
    k.weight = [k.sb(st, f"weight_of_choice{i}", [P, SEQ // P]) for i in range(2)]


def shared(k, st):
    k.hT = k.sb(st, "hT", [P, KD, TOK])
    k.region = k.sb(st, "region", [P, 12 * CW])
    k.half = k.sb(st, "half_region", [P, KB, SEQ])
    k.oT = k.sb(st, "oT", [P, KB, SEQ])

    def view(at, a, b):
        return k.region[:, at:at + a * b].rearrange("p (a b) -> p a b", a=a)

    k.w_mod = [view(KD * 512 * i, KD, 512) for i in range(3)]
    k.cT = view(0, 12, CW)
    k.qT, k.kT = view(0, HEADS, SEQ), view(HEADS * SEQ, HEADS, TOK)
    k.v = view(HEADS * (SEQ + TOK), TOK // P, BW)
    k.ybT, k.mT = view(0, KB, SEQ), view(KB * SEQ, KD, SEQ)
    k.w_out = [r[:, :, :].rearrange("p a n -> p (a n)").rearrange("p (c n) -> p c n", c=KD)
               for r in (k.half, k.oT)]
    k.zT, k.yaT, k.ycT = k.half, k.half, k.oT


def build(nc, dram):
    k = Core(nc, dram)
    scratch(nc, dram)
    with ExitStack() as st:
        allocate(k, st)
        with ExitStack() as st_shared:
            shared(k, st_shared)
            prepare(k)
            with ExitStack() as st_decay:
                k.beta = k.sb(st_decay, "beta", [P, TOK // P, 8])
                k.g = k.sb(st_decay, "decay", [P, TOK // P, 8])
                delta_in(k)
                delta(k)
            qkv(k)
            with ExitStack() as st_branches:
                k.brn_signals = Signals(nc, st_branches, "brn")
                k.pout_signals = Signals(nc, st_branches, "pout")
                k.w_b = [k.sb(st_branches, f"w_b{i}", [P, KD, P]) for i in range(2)]
                attend(k)
                branches(k)
                project_out(k)
        with ExitStack() as st_experts:
            k.exp_signals = Signals(nc, st_experts, "exp")
            k.w_gate = [k.sb(st_experts, f"w_gate{i}", [P, KD, D]) for i in range(2)]
            route(k)
            experts(k)
            combine(k)


def scratch(nc, dram):
    dram["x1"] = nc.dram_tensor("x1_rows", (SEQ, D), F32, kind="Internal").ap()
    dram["xn"] = nc.dram_tensor("xn_rows", (SEQ, D), F32, kind="Internal").ap()
    dram["tokens"] = nc.dram_tensor("block_tokens", (ROWS, 1), I32, kind="Internal").ap()
    dram["expert_rows"] = nc.dram_tensor("expert_rows", (ROWS, D), F32, kind="Internal").ap()


def kernel(**inputs):
    import concourse.bacc as bacc
    from concourse.bass_utils import run_bass_kernel_spmd

    nc = bacc.Bacc("TRN2", target_bir_lowering=False, num_devices=1)
    arrays, dram = {}, {}
    for name in INPUTS:
        arrays[f"in_{name}"] = np.ascontiguousarray(inputs[name])
    arrays["in_consts"], arrays["in_rope"] = constant_table(), rope_table()
    for name, a in arrays.items():
        dram[name[3:]] = nc.dram_tensor(name, a.shape, F32, kind="ExternalInput").ap()
    dram["out"] = nc.dram_tensor("out_0", (1, SEQ, D), F32, kind="ExternalOutput").ap()
    build(nc, dram)
    return run_bass_kernel_spmd(nc, [arrays], core_ids=[0]).results[0]["out_0"]
```
